# Optimizing a Trainium2 kernel written in Bass

```python
import jax, jax.numpy as jnp
from jax import lax
import numpy as np

D_MODEL = 1024
BATCH = 1
SEQ = 256
DEPTH = 2

CHUNK = 64
QBLK = 128
N_ATTN_HEADS = 8
ATTN_HEAD_DIM = 64
N_IDX_HEADS = 8
IDX_HEAD_DIM = 64
TOPK_MAX = 256
N_GLA_HEADS = 4
GLA_HEAD_K = 64
GLA_HEAD_V = 128
GLA_GATE_RANK = 16
GLA_GATE_TAU = 16.0
D_FF = 2816
PLE_DIM = 256
EPS = 1e-6

ATTN_W = N_ATTN_HEADS * ATTN_HEAD_DIM
IDX_Q_W = N_IDX_HEADS * IDX_HEAD_DIM
GLA_K_W = N_GLA_HEADS * GLA_HEAD_K
GLA_V_W = N_GLA_HEADS * GLA_HEAD_V
SPLIT_SIZES = (ATTN_W, ATTN_W, ATTN_W, IDX_Q_W, IDX_HEAD_DIM, N_IDX_HEADS,
               GLA_K_W, GLA_K_W, GLA_V_W, GLA_V_W, GLA_GATE_RANK, D_MODEL, D_MODEL)
W_IN = 5720

kernel_name = "hybrid_dsa_gla_macaron_ple"

def rmsnorm(x, g):
    xf = x.astype(jnp.float32)
    y = xf * lax.rsqrt(jnp.mean(xf * xf, axis=-1, keepdims=True) + EPS)
    return (y * g.astype(jnp.float32)).astype(x.dtype)

def swiglu(h, w_gate, w_up, w_down):
    return (jax.nn.silu(h @ w_gate) * (h @ w_up)) @ w_down

def dsa_attention(q, k, v, qi, ki, wi):
    B, S, H, Dh = q.shape
    topk = min(TOPK_MAX, S // 4)
    nblk = S // QBLK
    kchunk = jnp.arange(S) // CHUNK
    ki32 = ki.astype(jnp.float32)
    idx_scale = IDX_HEAD_DIM ** -0.5 * N_IDX_HEADS ** -0.5
    att_scale = Dh ** -0.5

    def block(i):
        start = i * QBLK
        qb = lax.dynamic_slice_in_dim(q, start, QBLK, axis=1)
        qib = lax.dynamic_slice_in_dim(qi, start, QBLK, axis=1).astype(jnp.float32)
        wib = lax.dynamic_slice_in_dim(wi, start, QBLK, axis=1).astype(jnp.float32)
        sc = jnp.einsum('bqhd,bsd->bqhs', qib, ki32)
        I = jnp.einsum('bqh,bqhs->bqs', wib * idx_scale, jax.nn.relu(sc))
        qchunk = (start + jnp.arange(QBLK)) // CHUNK
        adm = kchunk[None, :] <= qchunk[:, None]
        I = jnp.where(adm[None], I, -jnp.inf)
        vals, idx = lax.top_k(I, topk)
        valid = vals > -jnp.inf
        ksel = jax.vmap(lambda kk, ii: kk[ii])(k, idx)
        vsel = jax.vmap(lambda vv, ii: vv[ii])(v, idx)
        logits = jnp.einsum('bqhd,bqkhd->bqhk', qb, ksel).astype(jnp.float32) * att_scale
        logits = jnp.where(valid[:, :, None, :], logits, -jnp.inf)
        prob = jax.nn.softmax(logits, axis=-1).astype(v.dtype)
        return jnp.einsum('bqhk,bqkhd->bqhd', prob, vsel)

    out = lax.map(block, jnp.arange(nblk))
    return out.transpose(1, 0, 2, 3, 4).reshape(B, S, H, Dh)

def gla_chunked(q, k, v, logg):
    B, S, H, dk = q.shape
    dv = v.shape[-1]
    n = S // CHUNK

    def to_chunks(t):
        return t.astype(jnp.float32).reshape(B, n, CHUNK, H, t.shape[-1]).transpose(1, 0, 3, 2, 4)

    qc, kc, vc, gc = to_chunks(q * (dk ** -0.5)), to_chunks(k), to_chunks(v), to_chunks(logg)
    causal = jnp.tril(jnp.ones((CHUNK, CHUNK), dtype=bool))

    def step(state, inp):
        qb, kb, vb, gb = inp
        b = jnp.cumsum(gb, axis=2)
        o_inter = jnp.einsum('bhtd,bhde->bhte', qb * jnp.exp(b), state)
        diff = b[:, :, :, None, :] - b[:, :, None, :, :]
        decay = jnp.exp(jnp.where(causal[None, None, :, :, None], diff, -jnp.inf))
        attn = jnp.einsum('bhtd,bhsd,bhtsd->bhts', qb, kb, decay)
        o = o_inter + jnp.einsum('bhts,bhse->bhte', attn, vb)
        b_last = b[:, :, -1:, :]
        state = jnp.exp(b_last[:, :, 0, :])[..., None] * state + \
            jnp.einsum('bhsd,bhse->bhde', kb * jnp.exp(b_last - b), vb)
        return state, o

    state0 = jnp.zeros((B, H, dk, dv), jnp.float32)
    _, o = lax.scan(step, state0, (qc, kc, vc, gc))
    return o.transpose(1, 0, 3, 2, 4).reshape(B, S, H, dv).astype(v.dtype)

def token_mixer(h, w_in, gla_gate_w2, gla_gate_b, gla_norm, w_branch_a, w_branch_b, w_out):
    B, S, _ = h.shape
    z = h @ w_in
    cuts = np.cumsum(np.array(SPLIT_SIZES))[:-1].tolist()
    (aq, ak, av, iq, ik, iw, gq, gk, gv, gr, ga, mga, mgb) = jnp.split(z, cuts, axis=-1)
    hd = lambda t, nh: t.reshape(B, S, nh, -1)
    oa = dsa_attention(hd(aq, N_ATTN_HEADS), hd(ak, N_ATTN_HEADS), hd(av, N_ATTN_HEADS),
                       hd(iq, N_IDX_HEADS), ik, iw)
    ya = oa.reshape(B, S, ATTN_W) @ w_branch_a
    glog = jax.nn.log_sigmoid((ga @ gla_gate_w2 + gla_gate_b).astype(jnp.float32)) / GLA_GATE_TAU
    ob = gla_chunked(hd(gq, N_GLA_HEADS), hd(gk, N_GLA_HEADS), hd(gv, N_GLA_HEADS),
                     glog.reshape(B, S, N_GLA_HEADS, GLA_HEAD_K))
    ob = rmsnorm(ob, gla_norm).reshape(B, S, GLA_V_W) * jax.nn.silu(gr)
    yb = ob @ w_branch_b
    merged = jax.nn.sigmoid(mga) * ya + jax.nn.sigmoid(mgb) * yb
    return merged @ w_out

def setup_inputs(seed: int = 0) -> dict:
    key = jax.random.key(seed)
    ks = jax.random.split(key, 24)
    nrm = lambda k, shape, fan: jax.random.normal(k, shape, jnp.float32) * (fan ** -0.5)
    gain = lambda k, shape: 1.0 + 0.01 * jax.random.normal(k, shape, jnp.float32)
    L = DEPTH
    return {
        "x": jax.random.normal(ks[0], (BATCH, SEQ, D_MODEL), jnp.float32),
        "p": jax.random.normal(ks[1], (DEPTH, BATCH, SEQ, PLE_DIM), jnp.float32),
        "w_in": nrm(ks[2], (L, D_MODEL, W_IN), D_MODEL),
        "gla_gate_w2": nrm(ks[3], (L, GLA_GATE_RANK, GLA_K_W), GLA_GATE_RANK),
        "gla_gate_b": 0.1 * jax.random.normal(ks[4], (L, GLA_K_W), jnp.float32),
        "gla_norm": gain(ks[5], (L, GLA_HEAD_V)),
        "w_branch_a": nrm(ks[6], (L, ATTN_W, D_MODEL), ATTN_W),
        "w_branch_b": nrm(ks[7], (L, GLA_V_W, D_MODEL), GLA_V_W),
        "w_out": nrm(ks[8], (L, D_MODEL, D_MODEL), D_MODEL),
        "norm_ff1": gain(ks[9], (L, D_MODEL)),
        "norm_mix": gain(ks[10], (L, D_MODEL)),
        "norm_ff2": gain(ks[11], (L, D_MODEL)),
        "norm_ple": gain(ks[12], (L, D_MODEL)),
        "ff1_w_gate": nrm(ks[13], (L, D_MODEL, D_FF), D_MODEL),
        "ff1_w_up": nrm(ks[14], (L, D_MODEL, D_FF), D_MODEL),
        "ff1_w_down": nrm(ks[15], (L, D_FF, D_MODEL), D_FF),
        "ff2_w_gate": nrm(ks[16], (L, D_MODEL, D_FF), D_MODEL),
        "ff2_w_up": nrm(ks[17], (L, D_MODEL, D_FF), D_MODEL),
        "ff2_w_down": nrm(ks[18], (L, D_FF, D_MODEL), D_FF),
        "ple_w_proj": nrm(ks[19], (L, PLE_DIM, D_MODEL), PLE_DIM),
        "ple_w_gate": nrm(ks[20], (L, D_MODEL, D_MODEL), D_MODEL),
        "norm_final": gain(ks[21], (D_MODEL,)),
    }

def reference(x, p, w_in, gla_gate_w2, gla_gate_b, gla_norm, w_branch_a, w_branch_b, w_out,
              norm_ff1, norm_mix, norm_ff2, norm_ple, ff1_w_gate, ff1_w_up, ff1_w_down,
              ff2_w_gate, ff2_w_up, ff2_w_down, ple_w_proj, ple_w_gate, norm_final):
    for i in range(DEPTH):
        x = x + 0.5 * swiglu(rmsnorm(x, norm_ff1[i]), ff1_w_gate[i], ff1_w_up[i], ff1_w_down[i])
        x = x + token_mixer(rmsnorm(x, norm_mix[i]), w_in[i], gla_gate_w2[i], gla_gate_b[i],
                            gla_norm[i], w_branch_a[i], w_branch_b[i], w_out[i])
        x = x + 0.5 * swiglu(rmsnorm(x, norm_ff2[i]), ff2_w_gate[i], ff2_w_up[i], ff2_w_down[i])
        g = jax.nn.sigmoid(rmsnorm(x, norm_ple[i]) @ ple_w_gate[i])
        x = x + g * (p[i] @ ple_w_proj[i])
    return rmsnorm(x, norm_final)


_drawn_inputs = setup_inputs


def setup_inputs(seed=0):
    import zlib

    import numpy as np

    out = dict(_drawn_inputs(seed))
    spreads = {}
    factors = {'gla_gate_b': 3.043,
     'gla_norm': 8.0,
     'norm_ff1': 4.909,
     'norm_mix': 3.511,
     'norm_ff2': 8.0,
     'norm_ple': 8.0,
     'norm_final': 5.49}
    for name, (base, spread) in spreads.items():
        noise = np.random.default_rng([zlib.crc32(name.encode()), seed]).standard_normal(out[name].shape)
        drawn = base * np.exp(spread * noise) if base else spread * noise
        out[name] = __import__('jax').numpy.asarray(drawn.astype(out[name].dtype))
    for name, factor in factors.items():
        out[name] = (out[name] * factor).astype(out[name].dtype)
    return out
```

```python
from contextlib import ExitStack

import numpy as np

import concourse.bass as bass
from concourse import mybir

F32 = mybir.dt.float32
F32R = mybir.dt.float32r
ACT = mybir.ActivationFunctionType
ALU = mybir.AluOpType
AX_X = mybir.AxisListType.X

P = 128
EPS = 1e-6

N_FF = 11
FF1 = 0
MIX = 3 * N_FF
SMALL, IQ, GQ, GK, AQ, AK, AV, GV, GR = MIX, MIX + 1, MIX + 3, MIX + 4, MIX + 5, MIX + 7, MIX + 9, MIX + 11, MIX + 13
MGA, MGB, BRA, BRB, WOUT = MIX + 15, MIX + 19, MIX + 23, MIX + 25, MIX + 27
FF2 = WOUT + 4
PROJ = FF2 + 3 * N_FF
PGATE = PROJ + 1
CHUNKS = PGATE + 4
SLOTS = 3
TURNS = CHUNKS // SLOTS
assert CHUNKS % SLOTS == 0

COL = dict(aq=0, ak=512, av=1024, iq=1536, ik=2048, iw=2112, gq=2120, gk=2376, gv=2632, gr=3144, ga=3656,
           mga=3672, mgb=4696)
GA_ROW = 8

JOBS = ["wi", "small", "iq0", "iq1"] + [f"sc{j}" for j in range(8)] + [
    "gq", "gk", "glog", "aq0", "aq1", "ak0", "ak1", "av0", "av1", "gv0", "gv1", "kdT", "gr0", "gr1", "U0", "U1", "lg0"]
for _j in range(8):
    JOBS += [f"mg{_j}", f"pT{_j}"]
    JOBS += [f"lv{_j}0", f"lv{_j}1", f"lg{_j + 1}"] if _j < 7 else []
    JOBS += [f"oa{_j - 1}"] if _j else []
JOBS += ["oa7"] + [f"go{i}" for i in range(4)] + [f"ya{i}" for i in range(4)] + ["gT0", "gT1"] + [f"yb{i}" for i in range(4)]
MIX_BANKS = 6
BANK_OF = {j: i % MIX_BANKS for i, j in enumerate(JOBS)}
INDEX_OF = {j: i // MIX_BANKS for i, j in enumerate(JOBS)}
PER_BANK = [sum(1 for j in JOBS if BANK_OF[j] == b) for b in range(MIX_BANKS)]

BY_CHUNK = ("small", "iq", "gq", "gk", "aq", "ak", "av", "gv", "gr", "mg")
FILLED_JOBS = [j for j in JOBS if not j.startswith(BY_CHUNK) and j not in ("ya1", "ya3", "yb1", "yb3")]
FILLS = [sum(1 for j in FILLED_JOBS if BANK_OF[j] == b) for b in range(MIX_BANKS)]
FILL_OF = {j: sum(1 for i in FILLED_JOBS[:n + 1] if BANK_OF[i] == BANK_OF[j]) for n, j in enumerate(FILLED_JOBS)}

STEPS = [(qt, r, m) for qt in range(2) for r in range(2) for m in range(2)]
REPLACED = -3.3e38
INADMISSIBLE = -2.9e38
FAR = -1e30
VECTOR_STEPS, SCALAR_STEPS, POOL_STEPS = 64, 8, 10


def hybrid_trunk(nc, a, out):
    L_N, D, W_IN = a["w_in"].shape
    T = a["x"].shape[1]
    assert (T, D) == (256, 1024)
    with ExitStack() as ctx:
        def sb(name, shape, dt=F32):
            return ctx.enter_context(nc.sbuf_tensor(name, shape, dt))

        def sem(name):
            return ctx.enter_context(nc.semaphore(name))

        bank = [ctx.enter_context(nc.psum_tensor(f"bank{b}", [P, 512], F32)) for b in range(8)]

        x = sb("x", [P, 2, D])
        raw = sb("raw", [P, SLOTS, 2048])
        w_hi = sb("w_hi", [P, SLOTS, 2048], F32R)
        w_lo = sb("w_lo", [P, SLOTS, 2048], F32R)
        h_hi = sb("h_hi", [P, 8, T], F32R)
        h_lo = sb("h_lo", [P, 8, T], F32R)
        xn = sb("xn", [P, 2, D])
        gain = sb("gain", [P, D])
        ssq = sb("ssq", [P, 2])
        rstd = sb("rstd", [P, 2])
        small_hi = sb("small_hi", [P, 4, 512], F32R)
        small_lo = sb("small_lo", [P, 4, 512], F32R)
        silu = sb("silu", [P, 512])
        hidden = sb("hidden", [P, 2, 512])
        consts = sb("consts", [P, 8 * P + 512])
        iqT = sb("iqT", [P, 4, T])
        ikT = sb("ikT", [P, 2, T])
        w2 = sb("w2", [24, 256])
        gbias = sb("gbias", [P, 2])
        wi = sb("wi", [P, 2, 8])
        relu = sb("relu", [P, 2, 512])
        score = sb("score", [P, 2, T])
        top8 = sb("top8", [P, 8])
        selbias = sb("selbias", [P, 2, T])
        qT = sb("qT", [P, 4, T])
        kT = sb("kT", [P, 4, T])
        v = sb("v", [P, 2, 512])
        gqT = sb("gqT", [P, 512])
        gkT = sb("gkT", [P, 512])
        gv = sb("gv", [P, 2, 512])
        gsilu = sb("gsilu", [P, 2, 512])
        gnorm = sb("gnorm", [P, P])
        gate_a = sb("gate_a", [P, 8, T])
        gate_b = xn[:, :, :].rearrange("p a (b t) -> p (a b) t", t=T)
        proj = gate_a[:, :, :].rearrange("p a t -> p (a t)").rearrange("p (t n) -> p t n", t=2)
        mx = sb("mx", [P, 2, 2])
        nmx = sb("nmx", [P, 2, 2])
        psums = sb("psums", [P, 2, 2])
        rsum = sb("rsum", [P, 2, 2])
        dec = sb("dec", [P, 8])
        half_neg = sb("half_neg", [P, 8])
        prob = sb("prob", [P, 2, 512])
        probT = sb("probT", [P, 512])
        oa_hi, oa_lo = (b[:, 2:4, :].rearrange("p c n -> p (c n)").rearrange("p (k t) -> p k t", t=T)
                        for b in (small_hi, small_lo))
        obT_hi, obT_lo = (b[:, 0:2, :].rearrange("p c n -> p (c n)").rearrange("p (k t) -> p k t", t=T)
                          for b in (small_hi, small_lo))
        zg = silu
        decay_abs = hidden[:, 0, :]
        decay_ln = hidden[:, 1, :]
        bcum = sb("bcum", [P, 512])
        dist = sb("dist", [P, 512])
        lev = ikT[:, :, :].rearrange("p a t -> p (a t)")
        qlev = sb("qlev", [P, 512])
        klev = sb("klev", [P, 512])
        qdec = sb("qdec", [P, 512])
        kdT = silu
        state = sb("state", [P, 3, 2, P])
        masked = hidden
        amat = sb("amat", [P, 2, 512])
        go = iqT[:, :, :].rearrange("p a t -> p (a t)").rearrange("p (a t) -> p a t", a=2)
        gss = sb("gss", [P, 8])
        grstd = sb("grstd", [P, 8])
        p_in = go

        ident = consts[:, 0:P]
        reset = consts[:, 8 * P:8 * P + 512]

        landed = [sem(f"landed{s}") for s in range(SLOTS)]
        hi_ready = [sem(f"hi_ready{s}") for s in range(SLOTS)]
        lo_ready = [sem(f"lo_ready{s}") for s in range(SLOTS)]
        chunk_done = [sem(f"chunk_done{s}") for s in range(SLOTS)]
        extra_landed = sem("extra_landed")
        gain_landed = sem("gain_landed")
        const_landed = sem("const_landed")
        x_landed = sem("x_landed")
        layer_landed = sem("layer_landed")
        p_landed = sem("p_landed")
        w2_zeroed = sem("w2_zeroed")
        half_ready = sem("half_ready")
        gsilu_done = sem("gsilu_done")
        silu_done = sem("silu_done")
        hidden_done = sem("hidden_done")
        hidden_hi = sem("hidden_hi")
        hidden_lo = sem("hidden_lo")
        x_ready = sem("x_ready")
        ssq_done = sem("ssq_done")
        rstd_done = sem("rstd_done")
        xn_ready = sem("xn_ready")
        turned = [sem("turned0"), sem("turned1")]
        h_hi_ready = sem("h_hi_ready")
        h_lo_ready = sem("h_lo_ready")
        filled = [sem(f"filled{b}") for b in range(MIX_BANKS)]
        drained = [sem(f"drained{b}") for b in range(MIX_BANKS)]
        vector_step = sem("vector_step")
        scalar_step = sem("scalar_step")
        pool_step = sem("pool_step")
        selected = sem("selected")
        gla_scan = sem("gla_scan")
        gla_exp = sem("gla_exp")
        lev_dist = sem("lev_dist")
        lev_ready = sem("lev_ready")
        lev_used = sem("lev_used")
        masked_added = sem("masked_added")
        logit_ready = sem("logit_ready")
        prob_exp = sem("prob_exp")
        prob_ready = sem("prob_ready")
        oa_hi_ready = sem("oa_hi_ready")
        gss_done = sem("gss_done")
        grstd_done = sem("grstd_done")
        gT_hi_ready = sem("gT_hi_ready")
        scores_added = sem("scores_added")
        gr_tanh = sem("gr_tanh")
        merged = sem("merged")
        merged_hi = sem("merged_hi")
        merged_lo = sem("merged_lo")
        p_turned = sem("p_turned")
        pT_hi = sem("pT_hi")
        pT_lo = sem("pT_lo")
        proj_out = sem("proj_out")
        pgate_out = sem("pgate_out")
        final_done = sem("final_done")
        stored = sem("stored")
        pe_ticks, dve_ticks, pool_ticks, sp_ticks = (sem(f"{e}_ticks") for e in ("pe", "dve", "pool", "sp"))

        START = 1

        def start_counts(eng, sems):
            for s in sems:
                eng.sem_inc(s, START)

        def wait_stands_alone(eng, ticks):
            eng.sem_inc(ticks, 1)

        def turn(L, n, g=0):
            return n % SLOTS, L * TURNS + n // SLOTS + g + 1

        def wait_drained(eng, L, job):
            eng.wait_ge(drained[BANK_OF[job]], L * PER_BANK[BANK_OF[job]] + INDEX_OF[job] + 1 + START)

        def wait_filled(eng, L, job):
            eng.wait_ge(filled[BANK_OF[job]], L * FILLS[BANK_OF[job]] + FILL_OF[job])

        def wait_free(eng, L, job):
            eng.wait_ge(drained[BANK_OF[job]], L * PER_BANK[BANK_OF[job]] + INDEX_OF[job] + START)

        def raw_view(s, cols):
            return raw[:, s, :].rearrange("p (k n) -> p k n", n=cols)

        block = ctx.enter_context(nc.Block())

        @block.sync
        def _(sp):
            def slot_free(L, n, g=0):
                s, t = turn(L, n, g)
                sp.wait_ge(lo_ready[s], t - 1 + START)
                wait_stands_alone(sp, sp_ticks)
                return s

            def columns(L, n, w, c0, g=0):
                s = slot_free(L, n, g)
                src = w[L].rearrange("(k p) n -> p k n", p=P)
                src = src[:, :, c0:c0 + 256] if isinstance(c0, int) else src[:, :, bass.ds(c0, 256)]
                sp.dma_start(raw_view(s, 256), src).then_inc(landed[s], 16)

            def rows(L, n, w, k0, cols, c0=0, g=0):
                s = slot_free(L, n, g)
                k = 2048 // cols
                src = w[L].rearrange("(k p) n -> p k n", p=P)
                src = src[:, k0:k0 + k, c0:c0 + cols] if isinstance(k0, int) else src[:, bass.ds(k0, k), c0:c0 + cols]
                sp.dma_start(raw_view(s, cols), src).then_inc(landed[s], 16)

            def ffn(L, off, wg, wu, wd):
                columns(L, off, wg, 0)
                columns(L, off + 1, wu, 0)
                with sp.Fori(1, N_FF) as g:
                    columns(L, off - 1, wg, g * 256, g)
                    columns(L, off, wu, g * 256, g)
                    rows(L, off + 1, wd, g * 2 - 2, 1024, 0, g)
                rows(L, off + 3 * N_FF - 1, wd, 2 * N_FF - 2, 1024)

            def load_gain(L, k, name):
                sp.wait_ge(xn_ready, L * 8 + 2 * k + START)
                src = a[name][L].rearrange("(o n) -> o n", o=1).to_broadcast([P, D])
                sp.dma_start(gain[:, :], src).then_inc(gain_landed, 16)

            sp.dma_start(xn[:, :, :], a["x"][0].rearrange("(t p) n -> p t n", p=P)).then_inc(x_landed, 16)
            sp.dma_start(consts[:, :], a["consts"]).then_inc(const_landed, 16)
            with sp.Fori(0, L_N) as L:
                load_gain(L, 0, "norm_ff1")
                ffn(L, FF1, a["ff1_w_gate"], a["ff1_w_up"], a["ff1_w_down"])
                load_gain(L, 1, "norm_mix")
                sp.wait_ge(w2_zeroed, 1)
                sp.dma_start(w2[GA_ROW:GA_ROW + 16, :], a["gla_gate_w2"][L]).then_inc(layer_landed, 16)
                sp.dma_start(gbias[:, :], a["gla_gate_b"][L].rearrange("(c p) -> p c", p=P),
                             allow_slow_non_contiguous=True).then_inc(layer_landed, 16)
                sp.dma_start(gnorm[:, :], a["gla_norm"][L].rearrange("(o n) -> o n", o=1).to_broadcast([P, P])
                             ).then_inc(layer_landed, 16)
                s = slot_free(L, SMALL)
                w = a["w_in"][L].rearrange("(k p) n -> p k n", p=P)
                rv = raw_view(s, 256)
                sp.dma_start(rv[:, :, 0:64], w[:, :, COL["ik"]:COL["ik"] + 64]).then_inc(extra_landed, 16)
                sp.dma_start(rv[:, :, 64:136], w[:, :, COL["ik"]:COL["ik"] + 72]).then_inc(extra_landed, 16)
                sp.dma_start(rv[:, :, 136:256], w[:, :, COL["ga"]:COL["ga"] + 120]).then_inc(landed[s], 16)
                for n, c in [(IQ, "iq"), (IQ + 1, "iq"), (GQ, "gq"), (GK, "gk"), (AQ, "aq"), (AQ + 1, "aq"),
                             (AK, "ak"), (AK + 1, "ak")]:
                    first = dict(iq=IQ, gq=GQ, gk=GK, aq=AQ, ak=AK)[c]
                    columns(L, n, a["w_in"], COL[c] + 256 * (n - first))
                for first, c in [(AV, "av"), (GV, "gv"), (GR, "gr")]:
                    for i in range(2):
                        rows(L, first + i, a["w_in"], 4 * i, 512, COL[c])
                for i in range(8):
                    columns(L, MGA + i, a["w_in"], COL["mga"] + 256 * i)
                for i in range(2):
                    rows(L, BRA + i, a["w_branch_a"], 0, 512, 512 * i)
                for i in range(2):
                    rows(L, BRB + i, a["w_branch_b"], 0, 512, 512 * i)
                for i in range(4):
                    rows(L, WOUT + i, a["w_out"], 2 * i, 1024)
                load_gain(L, 2, "norm_ff2")
                ffn(L, FF2, a["ff2_w_gate"], a["ff2_w_up"], a["ff2_w_down"])
                load_gain(L, 3, "norm_ple")
                sp.dma_start(p_in[:, :, 0:256], a["p"][L, 0].rearrange("(t p) n -> p t n", p=P)).then_inc(p_landed, 16)
                rows(L, PROJ, a["ple_w_proj"], 0, 1024)
                for i in range(4):
                    rows(L, PGATE + i, a["ple_w_gate"], 2 * i, 1024)
            sp.wait_ge(xn_ready, L_N * 8 + START)
            sp.dma_start(gain[:, :], a["norm_final"].rearrange("(o n) -> o n", o=1).to_broadcast([P, D])
                         ).then_inc(gain_landed, 16)
            for t in range(2):
                sp.wait_ge(xn_ready, L_N * 8 + t + 1 + START)
                sp.dma_start(out[0, t * P:(t + 1) * P, :], xn[:, t, :]).then_inc(stored, 16)
            sp.wait_ge(stored, 32)

        @block.tensor
        def _(pe):
            def operands(L, n, g=0):
                s, t = turn(L, n, g)
                pe.wait_ge(lo_ready[s], t + START)
                return s

            def three(o, lh, ll, rh, rl, start, stop):
                pe.matmul(o, lh, rh, start=start, stop=False)
                pe.matmul(o, ll, rh, start=False, stop=False)
                return pe.matmul(o, lh, rl, start=False, stop=stop)

            def by_columns(s, o):
                wh, wl = (w[:, s, :].rearrange("p (k n) -> p k n", n=256) for w in (w_hi, w_lo))
                for c in range(2):
                    for k in range(8):
                        mm = three(o[:, c * T:(c + 1) * T], wh[:, k, c * P:(c + 1) * P], wl[:, k, c * P:(c + 1) * P],
                                   h_hi[:, k, :], h_lo[:, k, :], k == 0, k == 7)
                return mm.then_inc(chunk_done[s], 1)

            def by_tokens(s, o, xh, xl, cols, ks, first, last):
                wh, wl = (w[:, s, :].rearrange("p (k n) -> p k n", n=cols) for w in (w_hi, w_lo))
                for i, k in enumerate(ks):
                    for t in range(2):
                        for c in range(cols // 512):
                            cs = slice(c * 512, (c + 1) * 512)
                            mm = three(o(t, c), xh[:, k, t * P:(t + 1) * P], xl[:, k, t * P:(t + 1) * P],
                                       wh[:, i, cs], wl[:, i, cs], first and i == 0, last and i == len(ks) - 1)
                return mm.then_inc(chunk_done[s], 1)

            def acc(t, c):
                return bank[2 * t + c][:, :]

            def norm(L, k):
                for t in range(2):
                    pe.wait_ge(xn_ready, L * 8 + 2 * k + t + 1 + START)
                    for h in range(2):
                        if t == 1:
                            pe.wait_ge(h_lo_ready, L * 16 + 4 * k + h + 1)
                        for j in range(4):
                            kk = 4 * h + j
                            mm = pe.transpose(bank[6 + h][:, j * P:(j + 1) * P], xn[:, t, kk * P:(kk + 1) * P], ident)
                        mm.then_inc(turned[h], 1)

            def ffn(L, off, f):
                F = L * 22 + f * 11

                def gate(n, g, group):
                    s = operands(L, n, g)
                    pe.wait_ge(silu_done, F + group + START)
                    by_columns(s, bank[4])

                def up(n, g, group):
                    s = operands(L, n, g)
                    pe.wait_ge(hidden_done, F + group + START)
                    by_columns(s, bank[5])

                def down(n, g, group, par, first=False, last=False):
                    s = operands(L, n, g)
                    pe.wait_ge(hidden_lo, F + group + 1)
                    hh, hl = (b[:, par, :].rearrange("p (c t) -> p c t", t=T) for b in (small_hi, small_lo))
                    by_tokens(s, acc, hh, hl, 1024, range(2), first, last)

                pe.wait_ge(h_lo_ready, L * 16 + (4 if f == 0 else 12))
                gate(off, 0, 0)
                up(off + 1, 0, 0)
                gate(off + 2, 0, 1)
                up(off + 3, 0, 1)
                down(off + 4, 0, 0, 0, first=True)
                with pe.Fori(0, 4) as i:
                    for j in range(2):
                        g = i * 2 + j
                        gate(off + 5 + 3 * j, i * 2, g + 2)
                        up(off + 6 + 3 * j, i * 2, g + 2)
                        down(off + 7 + 3 * j, i * 2, g + 1, (j + 1) % 2)
                gate(off + 29, 0, 10)
                up(off + 30, 0, 10)
                down(off + 31, 0, 9, 1)
                down(off + 32, 0, 10, 0, last=True)

            def mix(L):
                def done(mm, name):
                    mm.then_inc(filled[BANK_OF[name]], 1)

                def chunk(n, name):
                    s = operands(L, n)
                    wait_free(pe, L, name)
                    by_columns(s, bank[BANK_OF[name]])
                    return s

                def scores(qT_, kT_, name, step):
                    qt, r, m = step
                    nk = P * (qt + 1)
                    rows = slice(64 * r, 64 * r + 64)
                    wait_free(pe, L, name)
                    for i in range(2):
                        mm = pe.matmul(bank[BANK_OF[name]][:, i * nk:(i + 1) * nk], qT_[rows, 2 * m + i, qt * P:(qt + 1) * P],
                                       kT_(rows, 2 * m + i, nk), start=True, stop=True)
                    done(mm, name)

                pe.wait_ge(h_lo_ready, L * 16 + 8)
                s = operands(L, SMALL)
                wait_free(pe, L, "wi")
                wh, wl = (w[:, s, :].rearrange("p (k n) -> p k n", n=256) for w in (w_hi, w_lo))
                for t in range(2):
                    for k in range(8):
                        mm = three(bank[BANK_OF["wi"]][:, t * 8:(t + 1) * 8], h_hi[:, k, t * P:(t + 1) * P],
                                   h_lo[:, k, t * P:(t + 1) * P], wh[:, k, P:P + 8], wl[:, k, P:P + 8], k == 0, k == 7)
                done(mm, "wi")
                chunk(SMALL, "small")
                chunk(IQ, "iq0")
                chunk(IQ + 1, "iq1")
                for job_ in ("small", "iq0", "iq1"):
                    wait_drained(pe, L, job_)
                for j in range(8):
                    scores(iqT, lambda rows, hp, nk: ikT[rows, 0, 0:nk], f"sc{j}", STEPS[j])
                chunk(GQ, "gq")
                chunk(GK, "gk")
                pe.wait_ge(layer_landed, (L + 1) * 48)
                wait_free(pe, L, "glog")
                for c in range(2):
                    mm = pe.matmul(bank[BANK_OF["glog"]][:, c * T:(c + 1) * T], w2[:, c * P:(c + 1) * P], ikT[0:24, 1, :],
                                   start=True, stop=True)
                done(mm, "glog")
                for i in range(2):
                    chunk(AQ + i, f"aq{i}")
                for i in range(2):
                    chunk(AK + i, f"ak{i}")
                for n, c in [(AV, "av"), (GV, "gv"), (GR, "gr")]:
                    for t in range(2):
                        wait_free(pe, L, f"{c}{t}")
                    for i in range(2):
                        s = operands(L, n + i)
                        by_tokens(s, lambda t, _: bank[BANK_OF[f"{c}{t}"]][:, :], h_hi, h_lo, 512,
                                  range(4 * i, 4 * i + 4), i == 0, i == 1)
                    if c == "gv":
                        pe.wait_ge(lev_ready, L * 8 + 1)
                        wait_free(pe, L, "kdT")
                        for q in range(4):
                            mm = pe.transpose(bank[BANK_OF["kdT"]][:, q * P:(q + 1) * P], klev[:, q * P:(q + 1) * P], ident)
                        done(mm, "kdT")
                wait_drained(pe, L, "kdT")
                wait_drained(pe, L, "gv1")
                for b, chunks in enumerate(((0, 2), (1,))):
                    wait_free(pe, L, f"U{b}")
                    wait_stands_alone(pe, pe_ticks)
                    for i, c in enumerate(chunks):
                        rows = slice(64 * (c % 2), 64 * (c % 2) + 64)
                        for pair in range(2):
                            for hh in range(2):
                                q = 2 * pair + c // 2
                                h = 2 * pair + hh
                                mm = pe.matmul(bank[BANK_OF[f"U{b}"]][64 * hh:64 * hh + 64, (2 * i + pair) * P:(2 * i + pair + 1) * P],
                                               kdT[rows, q * P + 64 * hh:q * P + 64 * hh + 64],
                                               gv[rows, c // 2, h * P:(h + 1) * P], start=True, stop=True)
                    done(mm, f"U{b}")

                def logits(j):
                    scores(qT, lambda rows, hp, nk: kT[rows, hp, 0:nk], f"lg{j}", STEPS[j])

                def turn_prob(j):
                    qt, r, m = STEPS[j]
                    name = f"pT{j}"
                    pe.wait_ge(prob_ready, L * 8 + j + 1)
                    wait_free(pe, L, name)
                    nb = qt + 1
                    for i in range(2):
                        for kt in range(nb):
                            q = i * nb + kt
                            mm = pe.transpose(bank[BANK_OF[name]][:, q * P:(q + 1) * P],
                                              prob[:, j % 2, i * nb * P + kt * P:i * nb * P + (kt + 1) * P], ident)
                    done(mm, name)

                def attend(j):
                    qt, r, m = STEPS[j]
                    name = f"oa{j}"
                    wait_drained(pe, L, f"pT{j}")
                    wait_free(pe, L, name)
                    nb = qt + 1
                    for i in range(2):
                        h = 2 * (2 * m + i) + r
                        for kt in range(nb):
                            q = i * nb + kt
                            mm = pe.matmul(bank[BANK_OF[name]][64 * r:64 * r + 64, i * P:(i + 1) * P],
                                           v[:, kt, h * 64:(h + 1) * 64], probT[:, q * P:(q + 1) * P],
                                           start=kt == 0, stop=kt == nb - 1)
                    done(mm, name)

                def level(l):
                    if l:
                        pe.wait_ge(lev_ready, L * 8 + 2 + l)
                    kk, qq = (gkT, gqT) if l == 0 else (klev, qlev)
                    for hh in range(2):
                        name = f"lv{l}{hh}"
                        wait_free(pe, L, name)
                        for q in range(4):
                            mm = pe.matmul(bank[BANK_OF[name]][:, q * P:(q + 1) * P], kk[64 * hh:64 * hh + 64, q * P:(q + 1) * P],
                                           qq[64 * hh:64 * hh + 64, q * P:(q + 1) * P], start=True, stop=True)
                        done(mm, name)

                for name in ("aq1", "ak1"):
                    wait_drained(pe, L, name)
                logits(0)
                for j in range(8):
                    chunk(MGA + j, f"mg{j}")
                    if j == 0:
                        wait_drained(pe, L, "av1")
                    turn_prob(j)
                    if j < 7:
                        level(j)
                        logits(j + 1)
                    if j >= 1:
                        attend(j - 1)
                attend(7)
                pe.wait_ge(masked_added, L * 12 + 12)
                assert BANK_OF["U0"] == BANK_OF["go0"]
                for t in range(2):
                    for hh in range(2):
                        name = f"go{2 * t + hh}"
                        wait_free(pe, L, name)
                        for pair in range(2):
                            h, q = 2 * pair + hh, 2 * pair + t
                            for c in (2 * t, 2 * t + 1):
                                o = bank[BANK_OF[name]][64 * (c % 2):64 * (c % 2) + 64, pair * P:(pair + 1) * P]
                                at = q * P + 64 * (c % 2)
                                mm = pe.matmul(o, amat[:, hh, at:at + 64], gv[:, t, h * P:(h + 1) * P],
                                               start=True, stop=c == 0)
                                if c:
                                    mm = pe.matmul(o, qdec[64 * hh:64 * hh + 64, at:at + 64],
                                                   state[64 * hh:64 * hh + 64, c - 1, pair, :], start=False, stop=True)
                        done(mm, name)
                def turn_gla():
                    for t in range(2):
                        name = f"gT{t}"
                        wait_drained(pe, L, f"go{2 * t}")
                        wait_drained(pe, L, f"go{2 * t + 1}")
                        if BANK_OF[name] != BANK_OF[f"go{2 * t + 1}"]:
                            wait_free(pe, L, name)
                        for h in range(4):
                            mm = pe.transpose(bank[BANK_OF[name]][:, h * P:(h + 1) * P], go[:, t, h * P:(h + 1) * P], ident)
                        done(mm, name)

                def branch(n, c, xh, xl):
                    for i in range(2):
                        s = operands(L, n + i)
                        wh, wl = (w[:, s, :].rearrange("p (k n) -> p k n", n=512) for w in (w_hi, w_lo))
                        for half in range(2):
                            name = f"{c}{2 * i + half}"
                            wait_free(pe, L, name)
                            for cc in range(2):
                                cs = slice((2 * half + cc) * P, (2 * half + cc + 1) * P)
                                for k in range(4):
                                    mm = three(bank[BANK_OF[name]][:, cc * T:(cc + 1) * T], wh[:, k, cs], wl[:, k, cs],
                                               xh[:, k, :], xl[:, k, :], k == 0, k == 3)
                            if half == 0:
                                done(mm, name)
                        mm.then_inc(chunk_done[s], 1)

                wait_drained(pe, L, "oa7")
                branch(BRA, "ya", oa_hi, oa_lo)
                turn_gla()
                wait_drained(pe, L, "gT0")
                wait_drained(pe, L, "gT1")
                branch(BRB, "yb", obT_hi, obT_lo)
                pe.wait_ge(merged_lo, L * 4 + 4)
                for i in range(4):
                    s = operands(L, WOUT + i)
                    by_tokens(s, acc, h_hi, h_lo, 1024, range(2 * i, 2 * i + 2), i == 0, i == 3)

            def embed(L):
                pe.wait_ge(p_landed, (L + 1) * 16)
                for k in range(2):
                    for t in range(2):
                        mm = pe.transpose(bank[4][:, k * T + t * P:k * T + (t + 1) * P], p_in[:, t, k * P:(k + 1) * P], ident)
                mm.then_inc(p_turned, 1)
                s = operands(L, PROJ)
                pe.wait_ge(pT_lo, L + 1)
                pe.wait_ge(x_ready, L * 8 + 8)
                wh, wl = (w[:, s, :].rearrange("p (k n) -> p k n", n=1024) for w in (w_hi, w_lo))
                ph, pl = (b[:, 0, :].rearrange("p (k t) -> p k t", t=T) for b in (small_hi, small_lo))
                for t in range(2):
                    for c in range(2):
                        for k in range(2):
                            mm = three(bank[2 * t + c][:, :], ph[:, k, t * P:(t + 1) * P], pl[:, k, t * P:(t + 1) * P],
                                       wh[:, k, c * 512:(c + 1) * 512], wl[:, k, c * 512:(c + 1) * 512], k == 0, k == 1)
                mm.then_inc(chunk_done[s], 1)
                norm(L, 3)
                pe.wait_ge(h_lo_ready, L * 16 + 16)
                pe.wait_ge(proj_out, L * 4 + 4)
                for i in range(4):
                    s = operands(L, PGATE + i)
                    by_tokens(s, acc, h_hi, h_lo, 1024, range(2 * i, 2 * i + 2), i == 0, i == 3)

            start_counts(pe, chunk_done)
            pe.wait_ge(const_landed, 16)
            with pe.Fori(0, L_N) as L:
                norm(L, 0)
                ffn(L, FF1, 0)
                norm(L, 1)
                mix(L)
                norm(L, 2)
                ffn(L, FF2, 1)
                embed(L)

        @block.scalar
        def _(act):
            steps = [0]

            def step(L, ins):
                ins.then_inc(scalar_step, 1)
                steps[0] += 1
                act.wait_ge(scalar_step, L * SCALAR_STEPS + steps[0])

            def split(L, n, g=0):
                s, t = turn(L, n, g)
                act.wait_ge(landed[s], t * 16)
                if n == SMALL:
                    act.wait_ge(extra_landed, (L + 1) * 32)
                act.wait_ge(chunk_done[s], t - 1 + START)
                act.activation(w_hi[:, s, :], raw[:, s, :], ACT.Copy).then_inc(hi_ready[s], 1)

            def chunk_products(L, n, g=0):
                s, t = turn(L, n, g)
                act.wait_ge(chunk_done[s], t + START)

            def squares(L, k):
                for t in range(2):
                    act.wait_ge(x_ready, L * 8 + 2 * k + t + 1)
                    act.activation(xn[:, t, :], x[:, t, :], ACT.Square, accum_out=ssq[:, t:t + 1]).then_inc(ssq_done, 1)

            def norm(L, k):
                squares(L, k)
                for t in range(2):
                    for h in range(2):
                        act.wait_ge(turned[h], L * 8 + 2 * k + t + 1)
                        act.activation(h_hi[:, 4 * h:4 * h + 4, t * P:(t + 1) * P],
                                       bank[6 + h][:, :].rearrange("p (k n) -> p k n", n=P), ACT.Copy).then_inc(h_hi_ready, 1)

            def ffn(L, off, f):
                F = L * 22 + f * 11

                def silu_gate(n, g, group):
                    chunk_products(L, n, g)
                    act.wait_ge(hidden_done, F + group + START)
                    act.activation(silu[:, :], bank[4][:, :], ACT.Silu).then_inc(silu_done, 1)

                def round_hidden(group, par):
                    act.wait_ge(hidden_done, F + group + 1 + START)
                    act.activation(small_hi[:, par, :], hidden[:, par, :], ACT.Copy).then_inc(hidden_hi, 1)

                split(L, off + 2)
                silu_gate(off, 0, 0)
                split(L, off + 3)
                round_hidden(0, 0)
                split(L, off + 4)
                silu_gate(off + 2, 0, 1)
                split(L, off + 5)
                round_hidden(1, 1)
                split(L, off + 6)
                split(L, off + 7)
                with act.Fori(0, 4) as i:
                    for j in range(2):
                        g = i * 2 + (j + 2)
                        silu_gate(off + 5 + 3 * j, i * 2, g)
                        split(L, off + 8 + 3 * j, i * 2)
                        chunk_products(L, off + 4 + 3 * j, i * 2)
                        round_hidden(g, j)
                        split(L, off + 9 + 3 * j, i * 2)
                        split(L, off + 10 + 3 * j, i * 2)
                silu_gate(off + 29, 0, 10)
                split(L, off + 32)
                chunk_products(L, off + 28)
                round_hidden(10, 0)
                split(L, off + 33)
                split(L, off + 34)

            def take(L, job, dst, func=ACT.Copy, scale=1.0, n=512):
                act.activation(dst, bank[BANK_OF[job]][:, 0:n], func, scale=scale).then_inc(drained[BANK_OF[job]], 1)

            def flat(t):
                return t.rearrange("p a b -> p (a b)")

            def mix(L):
                split(L, MIX + 2)
                wait_filled(act, L, "wi")
                take(L, "wi", flat(wi[:, :, :]), scale=float(64 ** -0.5 * 8 ** -0.5), n=16)
                chunk_products(L, SMALL)
                take(L, "small", flat(ikT[:, :, :]))
                split(L, MIX + 3)
                for i in range(2):
                    chunk_products(L, IQ + i)
                    take(L, f"iq{i}", flat(iqT[:, 2 * i:2 * i + 2, :]))
                    split(L, MIX + 4 + i)
                for j in range(8):
                    nk = P * (STEPS[j][0] + 1)
                    wait_filled(act, L, f"sc{j}")
                    if j >= 2:
                        act.wait_ge(scores_added, L * 8 + j - 1)
                    take(L, f"sc{j}", relu[:, j % 2, 0:2 * nk], ACT.Relu, n=2 * nk)
                chunk_products(L, GQ)
                take(L, "gq", gqT[:, :], scale=0.125)
                split(L, MIX + 6)
                chunk_products(L, GK)
                take(L, "gk", gkT[:, :])
                split(L, MIX + 7)
                wait_filled(act, L, "glog")
                act.wait_ge(layer_landed, (L + 1) * 48)
                zb = bank[BANK_OF["glog"]]
                act.activation(zg[:, 0:T], zb[:, 0:T], ACT.Identity, bias=gbias[:, 0:1])
                act.activation(zg[:, T:2 * T], zb[:, T:2 * T], ACT.Identity, bias=gbias[:, 1:2]).then_inc(drained[BANK_OF["glog"]], 1)
                wait_drained(act, L, "glog")
                step(L, act.activation(decay_abs, zg[:, :], ACT.Abs))
                step(L, act.activation(decay_ln, decay_abs, ACT.Exp, scale=-1.0))
                act.activation(decay_ln, decay_ln, ACT.Ln, bias=1.0).then_inc(gla_exp, 1)
                chunk_products(L, AQ)
                take(L, "aq0", flat(qT[:, 0:2, :]))
                split(L, MIX + 8)
                chunk_products(L, AQ + 1)
                take(L, "aq1", flat(qT[:, 2:4, :]))
                split(L, MIX + 9)
                act.wait_ge(gla_scan, L + 1)
                act.activation(qdec[:, :], bcum[:, :], ACT.Exp, scale=1.0 / 16)
                act.activation(dec[:, :], bcum[:, 63:512:64], ACT.Exp, scale=1.0 / 16).then_inc(gla_exp, 1)
                act.wait_ge(lev_dist, L * 7 + 1)
                act.activation(lev[:, :], dist[:, :], ACT.Exp, scale=-1.0 / 16).then_inc(gla_exp, 1)
                for i in range(2):
                    chunk_products(L, AK + i)
                    take(L, f"ak{i}", flat(kT[:, 2 * i:2 * i + 2, :]))
                    split(L, MIX + 10 + i)
                split(L, MIX + 12)
                chunk_products(L, AV + 1)
                for t in range(2):
                    take(L, f"av{t}", v[:, t, :])
                split(L, MIX + 13)
                split(L, MIX + 14)
                chunk_products(L, GV + 1)
                for t in range(2):
                    take(L, f"gv{t}", gv[:, t, :])
                split(L, MIX + 15)
                wait_filled(act, L, "kdT")
                take(L, "kdT", kdT[:, :])
                split(L, MIX + 16)
                chunk_products(L, GR + 1)
                for t in range(2):
                    act.activation(gsilu[:, t, :], bank[BANK_OF[f"gr{t}"]][:, :], ACT.Tanh, scale=0.5).then_inc(gr_tanh, 1)
                split(L, MIX + 17)

                def round_oa(j):
                    qt, r, m = STEPS[j]
                    rows = slice(64 * r, 64 * r + 64)
                    wait_filled(act, L, f"oa{j}")
                    act.activation(oa_hi[rows, 2 * m:2 * m + 2, qt * P:(qt + 1) * P],
                                   bank[BANK_OF[f"oa{j}"]][rows, 0:2 * P].rearrange("p (i q) -> p i q", i=2),
                                   ACT.Copy).then_inc(oa_hi_ready, 1)

                for j in range(8):
                    nk = P * (STEPS[j][0] + 1)
                    act.wait_ge(logit_ready, L * 8 + j + 1)
                    if j >= 2:
                        wait_filled(act, L, f"pT{j - 2}")
                    for i in range(2):
                        ins = act.activation(prob[:, j % 2, i * nk:(i + 1) * nk], relu[:, j % 2, i * nk:(i + 1) * nk], ACT.Exp,
                                             scale=0.125, bias=nmx[:, j % 2, i:i + 1], accum_out=psums[:, j % 2, i:i + 1])
                    ins.then_inc(prob_exp, 1)
                    if j < 6:
                        act.wait_ge(lev_dist, L * 7 + 2 + j)
                        act.wait_ge(lev_ready, L * 8 + 2 + j)
                        step(L, act.activation(lev[:, :], dist[:, :], ACT.Abs))
                        act.activation(lev[:, :], lev[:, :], ACT.Exp, scale=-1.0 / 16).then_inc(gla_exp, 1)
                    chunk_products(L, MGA + j)
                    gate = gate_a[:, 2 * j:2 * j + 2, :] if j < 4 else gate_b[:, 2 * j - 8:2 * j - 6, :]
                    take(L, f"mg{j}", flat(gate), ACT.Tanh, scale=0.5)
                    split(L, MGA + j + 3)
                    wait_filled(act, L, f"pT{j}")
                    if j >= 1:
                        wait_filled(act, L, f"oa{j - 1}")
                    take(L, f"pT{j}", probT[:, 0:2 * nk], n=2 * nk)
                    if j >= 1:
                        round_oa(j - 1)
                round_oa(7)
                for q in range(4):
                    t, hh = q // 2, q % 2
                    wait_filled(act, L, f"go{q}")
                    for pair in range(2):
                        h = 2 * pair + hh
                        ins = act.activation(go[:, t, h * P:(h + 1) * P], bank[BANK_OF[f"go{q}"]][:, pair * P:(pair + 1) * P],
                                             ACT.Square, accum_out=gss[:, 4 * t + h:4 * t + h + 1])
                    ins.then_inc(gss_done, 1)
                split(L, BRB + 1)
                split(L, WOUT)
                for t in range(2):
                    wait_filled(act, L, f"gT{t}")
                    act.activation(obT_hi[:, :, t * P:(t + 1) * P], bank[BANK_OF[f"gT{t}"]][:, :].rearrange("p (h t) -> p h t", h=4),
                                   ACT.Copy).then_inc(gT_hi_ready, 1)
                split(L, WOUT + 1)
                for i in range(4):
                    act.wait_ge(merged, L * 4 + i + 1)
                    act.activation(h_hi[:, 2 * i:2 * i + 2, :], gate_b[:, 2 * i:2 * i + 2, :], ACT.Copy).then_inc(merged_hi, 1)
                    if i == 1:
                        split(L, WOUT + 2)
                split(L, WOUT + 3)
                split(L, FF2)
                split(L, FF2 + 1)

            def embed(L):
                act.wait_ge(p_turned, L + 1)
                act.activation(small_hi[:, 0, :], bank[4][:, :], ACT.Copy).then_inc(pT_hi, 1)
                squares(L, 3)
                split(L, PROJ + 2)
                chunk_products(L, PROJ)
                for q in range(4):
                    act.activation(proj[:, q // 2, (q % 2) * 512:(q % 2 + 1) * 512], bank[q][:, :], ACT.Copy, scale=0.5
                                   ).then_inc(proj_out, 1)
                for t in range(2):
                    for h in range(2):
                        act.wait_ge(turned[h], L * 8 + 6 + t + 1)
                        act.activation(h_hi[:, 4 * h:4 * h + 4, t * P:(t + 1) * P],
                                       bank[6 + h][:, :].rearrange("p (k n) -> p k n", n=P), ACT.Copy).then_inc(h_hi_ready, 1)
                split(L, PGATE + 2)
                split(L, PGATE + 3)
                chunk_products(L, PGATE + 3)
                for q in range(4):
                    act.activation(xn[:, q // 2, (q % 2) * 512:(q % 2 + 1) * 512], bank[q][:, :], ACT.Tanh, scale=0.5
                                   ).then_inc(pgate_out, 1)

            start_counts(act, [silu_done] + drained)
            with act.Fori(0, L_N) as L:
                split(L, 0)
                split(L, 1)
                norm(L, 0)
                ffn(L, FF1, 0)
                norm(L, 1)
                mix(L)
                norm(L, 2)
                ffn(L, FF2, 1)
                embed(L)
            assert steps[0] == SCALAR_STEPS, steps
            squares(L_N, 0)

        @block.gpsimd
        def _(pool):
            steps = [0]

            def step(L, ins):
                ins.then_inc(pool_step, 1)
                steps[0] += 1
                pool.wait_ge(pool_step, L * POOL_STEPS + steps[0])

            def root(L, out_, sums, n, done, count=True):
                w = sums.shape[1]
                wait_stands_alone(pool, pool_ticks)
                ins = pool.tensor_scalar(out_, sums, 1.0 / n, EPS, ALU.mult, ALU.add)
                step(L, ins)
                pool.tensor_tensor(out_, out_, half_neg[:, 0:w], ALU.pow).then_inc(done, 1)

            def norm(L, k):
                for t in range(2):
                    pool.wait_ge(ssq_done, L * 8 + 2 * k + t + 1)
                    root(L, rstd[:, t:t + 1], ssq[:, t:t + 1], D, rstd_done)

            pool.memset(w2[:, :], 0.0).then_inc(w2_zeroed, 1)
            pool.memset(half_neg[:, :], -0.5).then_inc(half_ready, 1)
            pool.wait_ge(half_ready, 1)
            with pool.Fori(0, L_N) as L:
                norm(L, 0)
                norm(L, 1)
                pool.wait_ge(gla_exp, L * 9 + 3)
                wait_drained(pool, L, "gk")
                pool.tensor_tensor(klev[:, :], gkT[:, :], lev[:, :], ALU.mult).then_inc(lev_ready, 1)
                pool.tensor_tensor(qdec[:, :], gqT[:, :], qdec[:, :], ALU.mult).then_inc(lev_ready, 1)
                for j in range(7):
                    if j < 6:
                        pool.wait_ge(gla_exp, L * 9 + 4 + j)
                        wait_filled(pool, L, f"lv{j}1" if j else "kdT")
                        pool.tensor_tensor(klev[:, :], gkT[:, :], lev[:, :], ALU.mult)
                        pool.tensor_tensor(qlev[:, :], gqT[:, :], lev[:, :], ALU.mult).then_inc(lev_ready, 1)
                    if j:
                        for hh in range(2):
                            wait_drained(pool, L, f"lv{j}{hh}")
                            if j >= 2:
                                pool.wait_ge(masked_added, L * 12 + 2 * (j - 2) + hh + 1)
                            pool.tensor_tensor(amat[:, hh, :], amat[:, hh, :], masked[:, hh, :], ALU.add).then_inc(masked_added, 1)
                for t in range(2):
                    pool.wait_ge(gss_done, L * 4 + 2 * t + 2)
                    root(L, grstd[:, 4 * t:4 * t + 4], gss[:, 4 * t:4 * t + 4], P, grstd_done)
                norm(L, 2)
                norm(L, 3)
            assert steps[0] == POOL_STEPS, steps
            steps[0] = 0
            norm(L_N, 0)

        @block.vector
        def _(dve):
            steps = [0]

            def step(L, ins):
                ins.then_inc(vector_step, 1)
                steps[0] += 1
                dve.wait_ge(vector_step, L * VECTOR_STEPS + steps[0])

            def split(L, n, g=0):
                s, t = turn(L, n, g)
                dve.wait_ge(hi_ready[s], t)
                dve.tensor_tensor(w_lo[:, s, :], raw[:, s, :], w_hi[:, s, :].bitcast(F32), ALU.subtract).then_inc(lo_ready[s], 1)

            def chunk_products(L, n, g=0):
                s, t = turn(L, n, g)
                dve.wait_ge(chunk_done[s], t + START)

            def scaled_tiles(L, k, gains):
                dve.wait_ge(gain_landed, gains * 16)
                for t in range(2):
                    dve.wait_ge(rstd_done, L * 8 + 2 * k + t + 1)
                    dve.scalar_tensor_tensor(out=xn[:, t, :], in0=x[:, t, :], scalar=rstd[:, t:t + 1], in1=gain[:, :],
                                             op0=ALU.mult, op1=ALU.mult).then_inc(xn_ready, 1)

            def norm(L, k):
                scaled_tiles(L, k, L * 4 + k + 1)
                for t in range(2):
                    for h in range(2):
                        dve.wait_ge(h_hi_ready, L * 16 + 4 * k + 2 * t + h + 1)
                        hi = h_hi[:, 4 * h:4 * h + 4, t * P:(t + 1) * P]
                        dve.tensor_tensor(h_lo[:, 4 * h:4 * h + 4, t * P:(t + 1) * P],
                                          bank[6 + h][:, :].rearrange("p (k n) -> p k n", n=P), hi.bitcast(F32),
                                          ALU.subtract).then_inc(h_lo_ready, 1)

            def add_half(L, n, k):
                chunk_products(L, n)
                for q in range(4):
                    xs = x[:, q // 2, (q % 2) * 512:(q % 2 + 1) * 512]
                    ins = dve.scalar_tensor_tensor(out=xs, in0=bank[q][:, :], scalar=0.5, in1=xs, op0=ALU.mult, op1=ALU.add)
                    if q % 2:
                        ins.then_inc(x_ready, 1)

            def ffn(L, off, f):
                F = L * 22 + f * 11

                def gated(n, g, group, par):
                    chunk_products(L, n, g)
                    dve.wait_ge(silu_done, F + group + 1 + START)
                    dve.tensor_tensor(hidden[:, par, :], silu[:, :], bank[5][:, :], ALU.mult).then_inc(hidden_done, 1)

                def hidden_rest(group, par):
                    dve.wait_ge(hidden_hi, F + group + 1)
                    dve.tensor_tensor(small_lo[:, par, :], hidden[:, par, :], small_hi[:, par, :].bitcast(F32),
                                      ALU.subtract).then_inc(hidden_lo, 1)

                split(L, off + 2)
                gated(off + 1, 0, 0, 0)
                split(L, off + 3)
                hidden_rest(0, 0)
                split(L, off + 4)
                split(L, off + 5)
                gated(off + 3, 0, 1, 1)
                hidden_rest(1, 1)
                split(L, off + 6)
                split(L, off + 7)
                with dve.Fori(0, 4) as i:
                    for j in range(2):
                        g = i * 2 + (j + 2)
                        split(L, off + 8 + 3 * j, i * 2)
                        dve.wait_ge(hidden_lo, F + g - 1)
                        gated(off + 6 + 3 * j, i * 2, g, j)
                        hidden_rest(g, j)
                        split(L, off + 9 + 3 * j, i * 2)
                        split(L, off + 10 + 3 * j, i * 2)
                dve.wait_ge(hidden_lo, F + 9)
                gated(off + 30, 0, 10, 0)
                split(L, off + 32)
                hidden_rest(10, 0)
                split(L, off + 33)
                split(L, off + 34)

            def top_k(L, qt):
                nk = P * (qt + 1)
                sc = score[:, qt, 0:nk]
                step(L, dve.memset(score[0:64, qt, nk - 64:nk], INADMISSIBLE))
                for _ in range(8):
                    wait_stands_alone(dve, dve_ticks)
                    step(L, dve.max(top8[:, :], sc))
                    wait_stands_alone(dve, dve_ticks)
                    step(L, dve.match_replace(sc, top8[:, :], sc, REPLACED))
                dve.tensor_scalar(selbias[:, qt, 0:nk], sc, -3.0e38, FAR, ALU.is_ge, ALU.mult).then_inc(selected, 1)

            def mix(L):
                split(L, MIX + 2)
                split(L, MIX + 3)
                split(L, MIX + 4)
                split(L, MIX + 5)
                wait_drained(dve, L, "wi")
                for j in range(8):
                    qt, r, m = STEPS[j]
                    nk = P * (qt + 1)
                    wait_drained(dve, L, f"sc{j}")
                    for i in range(2):
                        h = 2 * (2 * m + i) + r
                        rl = relu[:, j % 2, i * nk:(i + 1) * nk]
                        sc = score[:, qt, 0:nk]
                        if j % 4 == 0 and i == 0:
                            ins = dve.tensor_scalar(sc, rl, wi[:, qt, h:h + 1], None, ALU.mult)
                        else:
                            ins = dve.scalar_tensor_tensor(out=sc, in0=rl, scalar=wi[:, qt, h:h + 1], in1=sc,
                                                           op0=ALU.mult, op1=ALU.add)
                        if i == 0:
                            step(L, ins)
                        else:
                            ins.then_inc(scores_added, 1)
                            dve.wait_ge(scores_added, L * 8 + j + 1)
                split(L, MIX + 6)
                top_k(L, 0)
                split(L, MIX + 7)
                dve.wait_ge(gla_exp, L * 9 + 1)
                step(L, dve.scalar_tensor_tensor(out=dist[:, :], in0=zg[:, :], scalar=0.0, in1=decay_ln,
                                                 op0=ALU.min, op1=ALU.subtract))
                dve.tensor_tensor_scan(bcum[:, :], reset, dist[:, :], 0.0, ALU.mult, ALU.add).then_inc(gla_scan, 1)
                split(L, MIX + 8)
                dve.wait_ge(gla_scan, L + 1)

                def distance(width, at):
                    b = bcum[:, :].rearrange("p (n w) -> p n w", w=width)
                    ref = b[:, :, at:at + 1].to_broadcast([P, 512 // width, width])
                    dve.tensor_tensor(dist[:, :].rearrange("p (n w) -> p n w", w=width), b, ref, ALU.subtract).then_inc(lev_dist, 1)

                distance(64, 63)
                split(L, MIX + 9)
                top_k(L, 1)
                split(L, MIX + 10)
                split(L, MIX + 11)
                split(L, MIX + 12)
                split(L, MIX + 13)
                split(L, MIX + 14)
                split(L, MIX + 15)
                split(L, MIX + 16)
                for t in range(2):
                    name = f"gr{t}"
                    dve.wait_ge(gr_tanh, L * 2 + t + 1)
                    dve.scalar_tensor_tensor(out=gsilu[:, t, :], in0=gsilu[:, t, :], scalar=1.0, in1=bank[BANK_OF[name]][:, :],
                                             op0=ALU.add, op1=ALU.mult).then_inc(drained[BANK_OF[name]], 1)
                for t in range(2):
                    wait_drained(dve, L, f"gr{t}")
                    g = gsilu[:, t, :].rearrange("p (h e) -> p h e", h=4)
                    gn = gnorm[:, :].unsqueeze(1).to_broadcast([P, 4, P])
                    dve.scalar_tensor_tensor(out=g, in0=g, scalar=0.5, in1=gn, op0=ALU.mult, op1=ALU.mult).then_inc(gsilu_done, 1)
                split(L, MIX + 17)

                u0 = bank[BANK_OF["U0"]][:, :].rearrange("p (c h e) -> p c h e", c=2, h=2)
                u1 = bank[BANK_OF["U1"]][:, 0:256].rearrange("p (h e) -> p h e", h=2)
                wait_filled(dve, L, "U0")
                wait_filled(dve, L, "U1")
                step(L, dve.tensor_copy(state[:, 0, :, :], u0[:, 0, :, :]))
                for c, u, job in [(1, u1, "U1"), (2, u0[:, 1, :, :], "U0")]:
                    for pair in range(2):
                        ins = dve.scalar_tensor_tensor(out=state[:, c, pair, :], in0=state[:, c - 1, pair, :],
                                                       scalar=dec[:, 4 * pair + c:4 * pair + c + 1], in1=u[:, pair, :],
                                                       op0=ALU.mult, op1=ALU.add)
                    ins.then_inc(drained[BANK_OF[job]], 1)
                    wait_drained(dve, L, job)

                def mask_logits(j):
                    qt = STEPS[j][0]
                    nk = P * (qt + 1)
                    name = f"lg{j}"
                    wait_filled(dve, L, name)
                    if j >= 2:
                        dve.wait_ge(prob_exp, L * 8 + j - 1)
                    lm = relu[:, j % 2, 0:2 * nk].rearrange("p (i k) -> p i k", i=2)
                    sel = selbias[:, qt:qt + 1, 0:nk].to_broadcast([P, 2, nk])
                    dve.tensor_tensor(lm, bank[BANK_OF[name]][:, 0:2 * nk].rearrange("p (i k) -> p i k", i=2), sel, ALU.add
                                      ).then_inc(drained[BANK_OF[name]], 1)
                    wait_drained(dve, L, name)
                    step(L, dve.tensor_reduce(mx[:, j % 2, :], lm, AX_X, ALU.max))
                    dve.tensor_scalar(nmx[:, j % 2, :], mx[:, j % 2, :], -0.125, None, ALU.mult).then_inc(logit_ready, 1)

                def normalise(j):
                    nk = P * (STEPS[j][0] + 1)
                    dve.wait_ge(prob_exp, L * 8 + j + 1)
                    step(L, dve.reciprocal(rsum[:, j % 2, :], psums[:, j % 2, :]))
                    for i in range(2):
                        pr = prob[:, j % 2, i * nk:(i + 1) * nk]
                        ins = dve.tensor_scalar(pr, pr, rsum[:, j % 2, i:i + 1], None, ALU.mult)
                    ins.then_inc(prob_ready, 1)

                def rest_oa(j):
                    qt, r, m = STEPS[j]
                    rows = slice(64 * r, 64 * r + 64)
                    dve.wait_ge(oa_hi_ready, L * 8 + j + 1)
                    at = (rows, slice(2 * m, 2 * m + 2), slice(qt * P, (qt + 1) * P))
                    dve.tensor_tensor(oa_lo[at], bank[BANK_OF[f"oa{j}"]][rows, 0:2 * P].rearrange("p (i q) -> p i q", i=2),
                                      oa_hi[at].bitcast(F32), ALU.subtract).then_inc(drained[BANK_OF[f"oa{j}"]], 1)

                dve.wait_ge(selected, L * 2 + 2)
                for j in range(8):
                    mask_logits(j)
                    if j < 6:
                        dve.wait_ge(gla_exp, L * 9 + 3 + j)
                        distance(2 << j, (1 << j) - 1)
                    normalise(j)
                    split(L, MGA + j + 3)
                    if j < 7:
                        for hh in range(2):
                            name = f"lv{j}{hh}"
                            wait_filled(dve, L, name)
                            if j >= 2:
                                dve.wait_ge(masked_added, L * 12 + 2 * (j - 2) + hh + 1)
                            dst = amat[:, hh, :] if j == 0 else masked[:, hh, :]
                            mask = consts[:, (1 + j) * P:(2 + j) * P].unsqueeze(1).to_broadcast([P, 4, P])
                            dve.tensor_tensor(dst.rearrange("p (q t) -> p q t", q=4),
                                              bank[BANK_OF[name]][:, :].rearrange("p (q t) -> p q t", q=4), mask, ALU.mult
                                              ).then_inc(drained[BANK_OF[name]], 1)
                    if j >= 1:
                        rest_oa(j - 1)
                rest_oa(7)
                dve.wait_ge(gsilu_done, L * 2 + 2)
                for t in range(2):
                    dve.wait_ge(grstd_done, L * 2 + t + 1)
                    for hh in range(2):
                        name = f"go{2 * t + hh}"
                        for pair in range(2):
                            h = 2 * pair + hh
                            ins = dve.scalar_tensor_tensor(out=go[:, t, h * P:(h + 1) * P],
                                                           in0=bank[BANK_OF[name]][:, pair * P:(pair + 1) * P],
                                                           scalar=grstd[:, 4 * t + h:4 * t + h + 1],
                                                           in1=gsilu[:, t, h * P:(h + 1) * P], op0=ALU.mult, op1=ALU.mult)
                        ins.then_inc(drained[BANK_OF[name]], 1)

                def gate_branch(c, i, gate):
                    name = f"{c}{i}"
                    if i % 2:
                        chunk_products(L, (BRA if c == "ya" else BRB) + i // 2)
                    else:
                        wait_filled(dve, L, name)
                    g = flat_(gate[:, 2 * i:2 * i + 2, :])
                    dve.scalar_tensor_tensor(out=g, in0=g, scalar=1.0, in1=bank[BANK_OF[name]][:, :],
                                             op0=ALU.add, op1=ALU.mult).then_inc(drained[BANK_OF[name]], 1)

                def flat_(t):
                    return t.rearrange("p a b -> p (a b)")

                gate_branch("ya", 0, gate_a)
                gate_branch("ya", 1, gate_a)
                split(L, BRB + 1)
                gate_branch("ya", 2, gate_a)
                gate_branch("ya", 3, gate_a)
                split(L, WOUT)
                for t in range(2):
                    dve.wait_ge(gT_hi_ready, L * 2 + t + 1)
                    name = f"gT{t}"
                    dve.tensor_tensor(obT_lo[:, :, t * P:(t + 1) * P], bank[BANK_OF[name]][:, :].rearrange("p (h t) -> p h t", h=4),
                                      obT_hi[:, :, t * P:(t + 1) * P].bitcast(F32), ALU.subtract
                                      ).then_inc(drained[BANK_OF[name]], 1)

                for i in range(4):
                    gate_branch("yb", i, gate_b)
                    wait_drained(dve, L, f"yb{i}")
                    ga, gb = gate_a[:, 2 * i:2 * i + 2, :], gate_b[:, 2 * i:2 * i + 2, :]
                    dve.tensor_tensor(flat_(gb), flat_(ga), flat_(gb), ALU.add).then_inc(merged, 1)
                    if i == 1:
                        split(L, WOUT + 1)
                    if i % 2:
                        for u in (i - 1, i):
                            dve.wait_ge(merged_hi, L * 4 + u + 1)
                            dve.tensor_tensor(h_lo[:, 2 * u:2 * u + 2, :], gate_b[:, 2 * u:2 * u + 2, :],
                                              h_hi[:, 2 * u:2 * u + 2, :].bitcast(F32), ALU.subtract).then_inc(merged_lo, 1)
                split(L, WOUT + 2)
                split(L, WOUT + 3)
                split(L, FF2)
                split(L, FF2 + 1)

            def embed(L):
                dve.wait_ge(pT_hi, L + 1)
                dve.tensor_tensor(small_lo[:, 0, :], bank[4][:, :], small_hi[:, 0, :].bitcast(F32), ALU.subtract).then_inc(pT_lo, 1)
                add_half(L, FF2 + 3 * N_FF - 1, 3)
                norm(L, 3)
                split(L, PROJ + 2)
                split(L, PGATE + 2)
                split(L, PGATE + 3)
                for q in range(4):
                    dve.wait_ge(pgate_out, L * 4 + q + 1)
                    cols = slice((q % 2) * 512, (q % 2 + 1) * 512)
                    g = xn[:, q // 2, cols]
                    step(L, dve.scalar_tensor_tensor(out=g, in0=g, scalar=1.0, in1=proj[:, q // 2, cols], op0=ALU.add, op1=ALU.mult))
                    ins = dve.tensor_tensor(x[:, q // 2, cols], x[:, q // 2, cols], g, ALU.add)
                    if q % 2:
                        ins.then_inc(x_ready, 1)

            start_counts(dve, lo_ready + [hidden_done, xn_ready])
            dve.wait_ge(x_landed, 16)
            dve.wait_ge(const_landed, 16)
            for t in range(2):
                dve.tensor_copy(x[:, t, :], xn[:, t, :]).then_inc(x_ready, 1)
            with dve.Fori(0, L_N) as L:
                split(L, 0)
                split(L, 1)
                norm(L, 0)
                ffn(L, FF1, 0)
                add_half(L, MIX - 1, 1)
                norm(L, 1)
                mix(L)
                add_half(L, FF2 - 1, 2)
                norm(L, 2)
                ffn(L, FF2, 1)
                embed(L)
            assert steps[0] == VECTOR_STEPS, steps
            scaled_tiles(L_N, 0, L_N * 4 + 1)


def constants():
    s, t = np.arange(P)[:, None], np.arange(P)[None, :]
    parts = [s == t, s == t]
    for level in range(1, 7):
        b = 1 << level
        parts.append((s // b == t // b) & (s % b < b // 2) & (t % b >= b // 2))
    parts.append(np.broadcast_to(np.arange(512) % 64 != 0, (P, 512)))
    return np.ascontiguousarray(np.concatenate(parts, axis=1).astype(np.float32))


INPUTS = ["x", "p", "w_in", "gla_gate_w2", "gla_gate_b", "gla_norm", "w_branch_a", "w_branch_b", "w_out", "norm_ff1",
          "norm_mix", "norm_ff2", "norm_ple", "ff1_w_gate", "ff1_w_up", "ff1_w_down", "ff2_w_gate", "ff2_w_up",
          "ff2_w_down", "ple_w_proj", "ple_w_gate", "norm_final"]


def kernel(**inputs):
    import concourse.bacc as bacc
    from concourse.bass_utils import run_bass_kernel_spmd

    nc = bacc.Bacc("TRN2", target_bir_lowering=False, num_devices=1)
    arrays = {name: np.ascontiguousarray(inputs[name]) for name in INPUTS}
    arrays["consts"] = constants()
    args = {name: nc.dram_tensor(f"in_{name}", v.shape, F32, kind="ExternalInput").ap() for name, v in arrays.items()}
    out = nc.dram_tensor("out", arrays["x"].shape, F32, kind="ExternalOutput").ap()
    hybrid_trunk(nc, args, out)
    r = run_bass_kernel_spmd(nc, [{f"in_{name}": v for name, v in arrays.items()}], core_ids=[0])
    return r.results[0]["out"]
```

```python
from contextlib import ExitStack

import numpy as np

import concourse.bass as bass
from concourse import mybir

F32 = mybir.dt.float32
F32R = mybir.dt.float32r
ACT = mybir.ActivationFunctionType
ALU = mybir.AluOpType
AX_X = mybir.AxisListType.X

P = 128
EPS = 1e-6

N_FF = 11
FF1 = 0
MIX = 3 * N_FF
AV, SMALL, IQ, GQ, GK, AQ, AK, GV, GR = MIX, MIX + 2, MIX + 3, MIX + 5, MIX + 6, MIX + 7, MIX + 9, MIX + 11, MIX + 13
MGA, MGB, BRA, BRB, WOUT = MIX + 15, MIX + 19, MIX + 23, MIX + 25, MIX + 27
FF2 = WOUT + 4
PROJ = FF2 + 3 * N_FF
PGATE = PROJ + 1
CHUNKS = PGATE + 4
SLOTS = 3
TURNS = CHUNKS // SLOTS
assert CHUNKS % SLOTS == 0

COL = dict(aq=0, ak=512, av=1024, iq=1536, ik=2048, iw=2112, gq=2120, gk=2376, gv=2632, gr=3144, ga=3656,
           mga=3672, mgb=4696)
GA_ROW = 8

JOBS = ["av0", "av1", "small", "iq0", "iq1", "wi"] + [f"sc{j}" for j in range(8)] + [
    "gq", "gk", "glog", "aq0", "aq1", "ak0", "ak1", "gv0", "gv1", "kdT", "lg0", "lg1", "gr0", "gr1", "U0", "U1"]
for _j in range(8):
    JOBS += [f"mg{_j}", f"pT{_j}"]
    JOBS += [f"lv{_j}0", f"lv{_j}1"] if _j < 7 else []
    JOBS += [f"lg{_j + 2}"] if _j < 6 else []
    JOBS += [f"oa{_j - 1}"] if _j else []
JOBS += ["go0", "go1", "oa7", "go2", "go3", "ya0", "ya1", "gT0", "gT1", "ya2", "ya3", "yb0", "yb1", "yb2", "yb3"]
MIX_BANKS = 6
BANK_OF = {j: i % MIX_BANKS for i, j in enumerate(JOBS)}
BANK_OF |= dict(yb0=4, yb1=5, yb2=4, yb3=5)
INDEX_OF = {j: sum(1 for i in JOBS[:n] if BANK_OF[i] == BANK_OF[j]) for n, j in enumerate(JOBS)}
PER_BANK = [sum(1 for j in JOBS if BANK_OF[j] == b) for b in range(MIX_BANKS)]
LAST_IN_BANK = [[j for j in JOBS if BANK_OF[j] == b][-1] for b in range(MIX_BANKS)]

BY_CHUNK = ("small", "iq", "gq", "gk", "aq", "ak", "av", "gv", "gr", "mg")
FILLED_JOBS = [j for j in JOBS if not j.startswith(BY_CHUNK) and j not in ("ya1", "ya3", "yb1", "yb3")]
FILLS = [sum(1 for j in FILLED_JOBS if BANK_OF[j] == b) for b in range(MIX_BANKS)]
FILL_OF = {j: sum(1 for i in FILLED_JOBS[:n + 1] if BANK_OF[i] == BANK_OF[j]) for n, j in enumerate(FILLED_JOBS)}

STEPS = [(qt, r, m) for qt in range(2) for r in range(2) for m in range(2)]
REPLACED = -3.3e38
INADMISSIBLE = -2.9e38
FAR = -1e30
VECTOR_STEPS, SCALAR_STEPS, POOL_STEPS = 64, 8, 18


def hybrid_trunk(nc, a, out):
    L_N, D, W_IN = a["w_in"].shape
    T = a["x"].shape[1]
    assert (T, D) == (256, 1024)
    with ExitStack() as ctx:
        def sb(name, shape, dt=F32):
            return ctx.enter_context(nc.sbuf_tensor(name, shape, dt))

        def sem(name):
            return ctx.enter_context(nc.semaphore(name))

        bank = [ctx.enter_context(nc.psum_tensor(f"bank{b}", [P, 512], F32)) for b in range(8)]

        x = sb("x", [P, 2, D])
        raw = sb("raw", [P, SLOTS, 2048])
        w_hi = sb("w_hi", [P, SLOTS, 2048], F32R)
        w_lo = sb("w_lo", [P, SLOTS, 2048], F32R)
        h_hi = sb("h_hi", [P, 8, T], F32R)
        h_lo = sb("h_lo", [P, 8, T], F32R)
        xn = sb("xn", [P, 2, D])
        gain = sb("gain", [P, D])
        ssq = sb("ssq", [P, 4])
        mean = sb("mean", [P, 2])
        rstd = sb("rstd", [P, 2])
        small_hi = sb("small_hi", [P, 4, 512], F32R)
        small_lo = sb("small_lo", [P, 4, 512], F32R)
        silu = sb("silu", [P, 512])
        hidden = sb("hidden", [P, 2, 512])
        consts = sb("consts", [P, P + 6 * 64 + 512])
        iqT = sb("iqT", [P, 4, T])
        ikT = sb("ikT", [P, 2, T])
        w2 = sb("w2", [24, 256])
        gbias = sb("gbias", [P, 2])
        wi = sb("wi", [P, 2, 8])
        relu = sb("relu", [P, 2, 512])
        score = sb("score", [P, 2, T])
        top8 = sb("top8", [P, 8])
        selbias = sb("selbias", [P, 2, T])
        qT = sb("qT", [P, 4, T])
        kT = sb("kT", [P, 4, T])
        v = sb("v", [P, 2, 512])
        gqT = sb("gqT", [P, 512])
        gkT = sb("gkT", [P, 512])
        gv = sb("gv", [P, 2, 512])
        gsilu = sb("gsilu", [P, 2, 512])
        gnorm = sb("gnorm", [P, P])
        gate_a = sb("gate_a", [P, 8, T])
        gate_b = xn[:, :, :].rearrange("p a (b t) -> p (a b) t", t=T)
        proj = gate_a[:, :, :].rearrange("p a t -> p (a t)").rearrange("p (t n) -> p t n", t=2)
        mx = sb("mx", [P, 2, 2])
        nmx = sb("nmx", [P, 2, 2])
        psums = sb("psums", [P, 2, 2])
        rsum = sb("rsum", [P, 2, 2])
        dec = sb("dec", [P, 8])
        half_neg = sb("half_neg", [P, 8])
        prob = sb("prob", [P, 2, 512])
        probT = sb("probT", [P, 512])
        oa_hi, oa_lo = (b[:, 2:4, :].rearrange("p c n -> p (c n)").rearrange("p (k t) -> p k t", t=T)
                        for b in (small_hi, small_lo))
        obT_hi, obT_lo = (b[:, 0:2, :].rearrange("p c n -> p (c n)").rearrange("p (k t) -> p k t", t=T)
                          for b in (small_hi, small_lo))
        pT_hi_, pT_lo_ = (b[:, 2, :].rearrange("p (k t) -> p k t", t=T) for b in (small_hi, small_lo))
        zg = silu
        decay_abs = hidden[:, 0, :]
        decay_ln = hidden[:, 1, :]
        bcum = sb("bcum", [P, 512])
        dist = sb("dist", [P, 512])
        lev = ikT[:, :, :].rearrange("p a t -> p (a t)")
        qlev = sb("qlev", [P, 512])
        klev = sb("klev", [P, 512])
        qdec = sb("qdec", [P, 512])
        kdT = silu
        state = sb("state", [P, 3, 2, P])
        masked = hidden
        amat = sb("amat", [P, 2, 512])
        go = iqT[:, :, :].rearrange("p a t -> p (a t)").rearrange("p (a t) -> p a t", a=2)
        gss = sb("gss", [P, 8])
        grstd = sb("grstd", [P, 8])
        p_in = go

        ident = consts[:, 0:P]
        reset = consts[:, P + 6 * 64:P + 6 * 64 + 512]

        landed = [sem(f"landed{s}") for s in range(SLOTS)]
        hi_ready = [sem(f"hi_ready{s}") for s in range(SLOTS)]
        lo_ready = [sem(f"lo_ready{s}") for s in range(SLOTS)]
        chunk_done = [sem(f"chunk_done{s}") for s in range(SLOTS)]
        extra_landed = sem("extra_landed")
        gain_landed = sem("gain_landed")
        const_landed = sem("const_landed")
        x_landed = [sem("x_landed0"), sem("x_landed1")]
        layer_landed = sem("layer_landed")
        p_landed = sem("p_landed")
        w2_zeroed = sem("w2_zeroed")
        half_ready = sem("half_ready")
        gsilu_done = sem("gsilu_done")
        silu_done = sem("silu_done")
        hidden_done = sem("hidden_done")
        hidden_turned = sem("hidden_turned")
        hidden_hi = sem("hidden_hi")
        hidden_lo = sem("hidden_lo")
        acc_ready = sem("acc_ready")
        proj_half = sem("proj_half")
        x_ready = sem("x_ready")
        ssq_done = sem("ssq_done")
        rstd_done = sem("rstd_done")
        xn_ready = sem("xn_ready")
        turned = [sem("turned0"), sem("turned1")]
        h_hi_ready = sem("h_hi_ready")
        h_lo_ready = sem("h_lo_ready")
        filled = [sem(f"filled{b}") for b in range(MIX_BANKS)]
        drained = [sem(f"drained{b}") for b in range(MIX_BANKS)]
        vector_step = sem("vector_step")
        scalar_step = sem("scalar_step")
        pool_step = sem("pool_step")
        selected = sem("selected")
        gla_scan = sem("gla_scan")
        gla_exp = sem("gla_exp")
        lev_dist = sem("lev_dist")
        lev_ready = sem("lev_ready")
        lev_used = sem("lev_used")
        masked_added = sem("masked_added")
        logit_ready = sem("logit_ready")
        prob_exp = sem("prob_exp")
        prob_ready = sem("prob_ready")
        oa_hi_ready = sem("oa_hi_ready")
        gss_done = sem("gss_done")
        grstd_done = sem("grstd_done")
        gT_hi_ready = sem("gT_hi_ready")
        scores_added = sem("scores_added")
        gr_tanh = sem("gr_tanh")
        merged = sem("merged")
        merged_hi = sem("merged_hi")
        merged_lo = sem("merged_lo")
        p_turned = sem("p_turned")
        pT_hi = sem("pT_hi")
        pT_lo = sem("pT_lo")
        proj_out = sem("proj_out")
        pgate_out = sem("pgate_out")
        final_done = sem("final_done")
        stored = sem("stored")
        pe_ticks, dve_ticks, pool_ticks, sp_ticks = (sem(f"{e}_ticks") for e in ("pe", "dve", "pool", "sp"))

        START = 1

        def start_counts(eng, sems):
            for s in sems:
                eng.sem_inc(s, START)

        def wait_stands_alone(eng, ticks):
            eng.sem_inc(ticks, 1)

        def turn(L, n, g=0):
            return n % SLOTS, L * TURNS + n // SLOTS + g + 1

        def wait_drained(eng, L, job):
            eng.wait_ge(drained[BANK_OF[job]], L * PER_BANK[BANK_OF[job]] + INDEX_OF[job] + 1 + START)

        def wait_filled(eng, L, job):
            eng.wait_ge(filled[BANK_OF[job]], L * FILLS[BANK_OF[job]] + FILL_OF[job])

        def wait_free(eng, L, job):
            eng.wait_ge(drained[BANK_OF[job]], L * PER_BANK[BANK_OF[job]] + INDEX_OF[job] + START)

        def raw_view(s, cols):
            return raw[:, s, :].rearrange("p (k n) -> p k n", n=cols)

        block = ctx.enter_context(nc.Block())

        @block.sync
        def _(sp):
            def slot_free(L, n, g=0):
                s, t = turn(L, n, g)
                sp.wait_ge(lo_ready[s], t - 1 + START)
                wait_stands_alone(sp, sp_ticks)
                return s

            def columns(L, n, w, c0, g=0, source=None):
                s = slot_free(L, n, g)
                src = w[L if source is None else source].rearrange("(k p) n -> p k n", p=P)
                src = src[:, :, c0:c0 + 256] if isinstance(c0, int) else src[:, :, bass.ds(c0, 256)]
                sp.dma_start(raw_view(s, 256), src).then_inc(landed[s], 16)

            def rows(L, n, w, k0, cols, c0=0, g=0):
                s = slot_free(L, n, g)
                k = 2048 // cols
                src = w[L].rearrange("(k p) n -> p k n", p=P)
                src = src[:, k0:k0 + k, c0:c0 + cols] if isinstance(k0, int) else src[:, bass.ds(k0, k), c0:c0 + cols]
                sp.dma_start(raw_view(s, cols), src).then_inc(landed[s], 16)

            def ffn(L, off, wg, wu, wd):
                if off:
                    columns(L, off, wg, 0)
                columns(L, off + 1, wu, 0)
                with sp.Fori(1, N_FF) as g:
                    columns(L, off - 1, wg, g * 256, g)
                    columns(L, off, wu, g * 256, g)
                    rows(L, off + 1, wd, g * 2 - 2, 1024, 0, g)
                rows(L, off + 3 * N_FF - 1, wd, 2 * N_FF - 2, 1024)

            def load_gain(L, k, gains):
                sp.wait_ge(xn_ready, L * 16 + 4 * k + START)
                sp.dma_start(gain[:, :], gains.rearrange("(o n) -> o n", o=1).to_broadcast([P, D])).then_inc(gain_landed, 16)

            def load_x(t):
                sp.dma_start(x[:, t, :], a["x"][0, t * P:(t + 1) * P, :]).then_inc(x_landed[t], 16)

            def layer(L, last):
                ffn(L, FF1, a["ff1_w_gate"], a["ff1_w_up"], a["ff1_w_down"])
                load_gain(L, 1, a["norm_mix"][L])
                sp.wait_ge(w2_zeroed, 1)
                sp.dma_start(consts[:, P:], a["consts"][:, P:]).then_inc(layer_landed, 16)
                sp.dma_start(w2[GA_ROW:GA_ROW + 16, :], a["gla_gate_w2"][L]).then_inc(layer_landed, 16)
                sp.dma_start(gbias[:, :], a["gla_gate_b"][L].rearrange("(c p) -> p c", p=P),
                             allow_slow_non_contiguous=True).then_inc(layer_landed, 16)
                sp.dma_start(gnorm[:, :], a["gla_norm"][L].rearrange("(o n) -> o n", o=1).to_broadcast([P, P])
                             ).then_inc(layer_landed, 16)
                for i in range(2):
                    rows(L, AV + i, a["w_in"], 4 * i, 512, COL["av"])
                s = slot_free(L, SMALL)
                w = a["w_in"][L].rearrange("(k p) n -> p k n", p=P)
                rv = raw_view(s, 256)
                sp.dma_start(rv[:, :, 0:64], w[:, :, COL["ik"]:COL["ik"] + 64]).then_inc(extra_landed, 16)
                sp.dma_start(rv[:, :, 64:136], w[:, :, COL["ik"]:COL["ik"] + 72]).then_inc(extra_landed, 16)
                sp.dma_start(rv[:, :, 136:256], w[:, :, COL["ga"]:COL["ga"] + 120]).then_inc(landed[s], 16)
                for n, c in [(IQ, "iq"), (IQ + 1, "iq"), (GQ, "gq"), (GK, "gk"), (AQ, "aq"), (AQ + 1, "aq"),
                             (AK, "ak"), (AK + 1, "ak")]:
                    first = dict(iq=IQ, gq=GQ, gk=GK, aq=AQ, ak=AK)[c]
                    columns(L, n, a["w_in"], COL[c] + 256 * (n - first))
                for first, c in [(GV, "gv"), (GR, "gr")]:
                    for i in range(2):
                        rows(L, first + i, a["w_in"], 4 * i, 512, COL[c])
                for i in range(8):
                    columns(L, MGA + i, a["w_in"], COL["mga"] + 256 * i)
                for i in range(2):
                    rows(L, BRA + i, a["w_branch_a"], 0, 512, 512 * i)
                for i in range(2):
                    rows(L, BRB + i, a["w_branch_b"], 0, 512, 512 * i)
                for i in range(4):
                    rows(L, WOUT + i, a["w_out"], 2 * i, 1024)
                load_gain(L, 2, a["norm_ff2"][L])
                sp.dma_start(p_in[:, :, 0:256], a["p"][L, 0].rearrange("(t p) n -> p t n", p=P)).then_inc(p_landed, 16)
                ffn(L, FF2, a["ff2_w_gate"], a["ff2_w_up"], a["ff2_w_down"])
                load_gain(L, 3, a["norm_ple"][L])
                rows(L, PROJ, a["ple_w_proj"], 0, 1024)
                for i in range(4):
                    rows(L, PGATE + i, a["ple_w_gate"], 2 * i, 1024)
                if last:
                    load_gain(L, 4, a["norm_final"])
                else:
                    columns(L, CHUNKS, a["ff1_w_gate"], 0, source=L + 1)
                    load_gain(L, 4, a["norm_ff1"][L + 1])

            load_x(0)
            columns(0, 0, a["ff1_w_gate"], 0)
            load_gain(0, 0, a["norm_ff1"][0])
            sp.dma_start(ident, a["consts"][:, 0:P]).then_inc(const_landed, 16)
            load_x(1)
            with sp.Fori(0, L_N - 1) as L:
                layer(L, False)
            layer(L_N - 1, True)
            for t in range(2):
                for c in range(2):
                    sp.wait_ge(xn_ready, L_N * 16 + 2 * t + c + 1 + START)
                    sp.dma_start(out[0, t * P:(t + 1) * P, c * 512:(c + 1) * 512], xn[:, t, c * 512:(c + 1) * 512]
                                 ).then_inc(stored, 16)
            sp.wait_ge(stored, 64)

        @block.tensor
        def _(pe):
            def operands(L, n, g=0):
                s, t = turn(L, n, g)
                pe.wait_ge(lo_ready[s], t + START)
                return s

            def three(o, lh, ll, rh, rl, start, stop):
                pe.matmul(o, lh, rh, start=start, stop=False)
                pe.matmul(o, ll, rh, start=False, stop=False)
                return pe.matmul(o, lh, rl, start=False, stop=stop)

            def by_columns(s, o):
                wh, wl = (w[:, s, :].rearrange("p (k n) -> p k n", n=256) for w in (w_hi, w_lo))
                for c in range(2):
                    for k in range(8):
                        mm = three(o[:, c * T:(c + 1) * T], wh[:, k, c * P:(c + 1) * P], wl[:, k, c * P:(c + 1) * P],
                                   h_hi[:, k, :], h_lo[:, k, :], k == 0, k == 7)
                mm.then_inc(chunk_done[s], 1)

            def by_tokens(s, o, xh, xl, cols, ks, first, last):
                wh, wl = (w[:, s, :].rearrange("p (k n) -> p k n", n=cols) for w in (w_hi, w_lo))
                for i, k in enumerate(ks):
                    for t in range(2):
                        for c in range(cols // 512):
                            cs = slice(c * 512, (c + 1) * 512)
                            mm = three(o(t, c), xh[:, k, t * P:(t + 1) * P], xl[:, k, t * P:(t + 1) * P],
                                       wh[:, i, cs], wl[:, i, cs], first and i == 0, last and i == len(ks) - 1)
                return mm.then_inc(chunk_done[s], 1)

            def acc(t, c):
                return bank[2 * t + c][:, :]

            def tokens_of(L, ns, ks, t, xh, xl, first, last, between={}):
                at = 0
                for i, (n, kk) in enumerate(zip(ns, ks)):
                    s, _ = turn(L, n)
                    wh, wl = (w[:, s, :].rearrange("p (k n) -> p k n", n=1024) for w in (w_hi, w_lo))
                    for b, k in enumerate(kk):
                        for c in range(2):
                            if at in between:
                                between[at]()
                            at += 1
                            cs = slice(c * 512, (c + 1) * 512)
                            mm = three(bank[2 * t + c][:, :], xh(k)[:, t * P:(t + 1) * P], xl(k)[:, t * P:(t + 1) * P],
                                       wh[:, b, cs], wl[:, b, cs], first and i == 0 and b == 0,
                                       last and i == len(ns) - 1 and b == len(kk) - 1)
                    if t == 1:
                        mm.then_inc(chunk_done[s], 1)
                    elif last and i == len(ns) - 1:
                        mm.then_inc(acc_ready, 1)

            def turn_half(L, k, t, h):
                pe.wait_ge(xn_ready, L * 16 + 4 * k + 2 * t + h + 1 + START)
                if t == 1:
                    pe.wait_ge(h_lo_ready, L * 16 + 4 * k + h + 1)
                for j in range(4):
                    kk = 4 * h + j
                    mm = pe.transpose(bank[6 + h][:, j * P:(j + 1) * P], xn[:, t, kk * P:(kk + 1) * P], ident)
                mm.then_inc(turned[h], 1)

            def turning(L, k, t, ahead_of):
                return {at: (lambda h=h: turn_half(L, k, t, h)) for h, at in enumerate(ahead_of)}

            def first_two(L, k, n, outs, cols):
                def product(i, t, between={}):
                    ready = L * 16 + 4 * k + 2 * t
                    s = operands(L, n + i) if t == 0 else turn(L, n + i)[0]
                    wh, wl = (w[:, s, :].rearrange("p (k n) -> p k n", n=cols) for w in (w_hi, w_lo))
                    ks = range(8) if cols == 256 else range(4 * i, 4 * i + 4)
                    for b, kk in enumerate(ks):
                        if b in between:
                            between[b]()
                        if i == 0 and b == 0:
                            pe.wait_ge(h_lo_ready, ready + 1)
                        if kk == 4 and i == (cols == 512):
                            pe.wait_ge(h_lo_ready, ready + 2)
                        tokens = slice(t * P, (t + 1) * P)
                        mm = three(outs(i, t), h_hi[:, kk, tokens], h_lo[:, kk, tokens], wh[:, b, :], wl[:, b, :],
                                   kk == 0, kk == 7)
                    if t == 1:
                        mm.then_inc(chunk_done[s], 1)

                product(0, 0)
                product(1, 0, turning(L, k, 1, (3, 6) if cols == 256 else (1, 3)))
                product(0, 1)
                product(1, 1)

            def turn_embedding(L):
                pe.wait_ge(p_landed, (L + 1) * 16)
                for k in range(2):
                    for t in range(2):
                        mm = pe.transpose(bank[6][:, k * T + t * P:k * T + (t + 1) * P], p_in[:, t, k * P:(k + 1) * P], ident)
                mm.then_inc(p_turned, 1)

            def ffn(L, off, f):
                F = L * 22 + f * 11

                def gate(n, g, group):
                    s = operands(L, n, g)
                    pe.wait_ge(silu_done, F + group + START)
                    by_columns(s, bank[4])

                def up(n, g, group):
                    s = operands(L, n, g)
                    pe.wait_ge(hidden_done, F + group + START)
                    by_columns(s, bank[5])

                def down(n, g, group, par, first=False, last=False):
                    s = operands(L, n, g)
                    pe.wait_ge(hidden_lo, F + group + 1)
                    hh, hl = (b[:, par, :].rearrange("p (c t) -> p c t", t=T) for b in (small_hi, small_lo))
                    by_tokens(s, acc, hh, hl, 1024, range(2), first, last)

                first_two(L, 2 * f, off, lambda i, t: bank[4 + i][:, t * 256:(t + 1) * 256], 256)
                gate(off + 2, 0, 1)
                pe.wait_ge(hidden_done, F + 1 + START)
                for c in range(2):
                    for t in range(2):
                        mm = pe.transpose(bank[6][:, c * T + t * P:c * T + (t + 1) * P],
                                          hidden[:, 0, t * 256 + c * P:t * 256 + (c + 1) * P], ident)
                mm.then_inc(hidden_turned, 1)
                up(off + 3, 0, 1)
                down(off + 4, 0, 0, 0, first=True)
                with pe.Fori(0, 4) as i:
                    for j in range(2):
                        g = i * 2 + j
                        gate(off + 5 + 3 * j, i * 2, g + 2)
                        up(off + 6 + 3 * j, i * 2, g + 2)
                        down(off + 7 + 3 * j, i * 2, g + 1, (j + 1) % 2)
                gate(off + 29, 0, 10)
                up(off + 30, 0, 10)
                if f == 1:
                    turn_embedding(L)
                hidden_of = [b.rearrange("p g (c t) -> p (g c) t", t=T) for b in (small_hi, small_lo)]
                operands(L, off + 31)
                pe.wait_ge(hidden_lo, F + 10)
                for t in range(2):
                    if t == 0:
                        tokens_of(L, [off + 31], [(2, 3)], 0, *[lambda k, b=b: b[:, k, :] for b in hidden_of], False, False)
                        operands(L, off + 32)
                        pe.wait_ge(hidden_lo, F + 11)
                        tokens_of(L, [off + 32], [(0, 1)], 0, *[lambda k, b=b: b[:, k, :] for b in hidden_of], False, True)
                    else:
                        tokens_of(L, [off + 31, off + 32], [(2, 3), (0, 1)], 1,
                                  *[lambda k, b=b: b[:, k, :] for b in hidden_of], False, True,
                                  turning(L, 1, 0, (6, 7)) if f == 0 else {})

            def mix(L):
                def done(mm, name):
                    mm.then_inc(filled[BANK_OF[name]], 1)

                def chunk(n, name):
                    s = operands(L, n)
                    wait_free(pe, L, name)
                    by_columns(s, bank[BANK_OF[name]])
                    return s

                def scores(qT_, kT_, name, step):
                    qt, r, m = step
                    nk = P * (qt + 1)
                    rows = slice(64 * r, 64 * r + 64)
                    wait_free(pe, L, name)
                    for i in range(2):
                        mm = pe.matmul(bank[BANK_OF[name]][:, i * nk:(i + 1) * nk], qT_[rows, 2 * m + i, qt * P:(qt + 1) * P],
                                       kT_(rows, 2 * m + i, nk), start=True, stop=True)
                    done(mm, name)

                for t in range(2):
                    wait_free(pe, L, f"av{t}")
                first_two(L, 1, AV, lambda i, t: bank[BANK_OF[f"av{t}"]][:, :], 512)
                chunk(SMALL, "small")
                chunk(IQ, "iq0")
                chunk(IQ + 1, "iq1")
                wait_drained(pe, L, "small")
                wait_free(pe, L, "wi")
                for t in range(2):
                    mm = pe.transpose(bank[BANK_OF["wi"]][:, t * P:(t + 1) * P], ikT[:, 1, t * P:(t + 1) * P], ident)
                done(mm, "wi")
                for job_ in ("iq0", "iq1"):
                    wait_drained(pe, L, job_)
                for j in range(8):
                    scores(iqT, lambda rows, hp, nk: ikT[rows, 0, 0:nk], f"sc{j}", STEPS[j])
                chunk(GQ, "gq")
                chunk(GK, "gk")
                pe.wait_ge(layer_landed, (L + 1) * 64)
                wait_free(pe, L, "glog")
                for c in range(2):
                    mm = pe.matmul(bank[BANK_OF["glog"]][:, c * T:(c + 1) * T], w2[:, c * P:(c + 1) * P], ikT[0:24, 1, :],
                                   start=True, stop=True)
                done(mm, "glog")
                for i in range(2):
                    chunk(AQ + i, f"aq{i}")
                for i in range(2):
                    chunk(AK + i, f"ak{i}")
                def logits(j):
                    scores(qT, lambda rows, hp, nk: kT[rows, hp, 0:nk], f"lg{j}", STEPS[j])

                for n, c in [(GV, "gv"), (GR, "gr")]:
                    for t in range(2):
                        wait_free(pe, L, f"{c}{t}")
                    for i in range(2):
                        s = operands(L, n + i)
                        by_tokens(s, lambda t, _: bank[BANK_OF[f"{c}{t}"]][:, :], h_hi, h_lo, 512,
                                  range(4 * i, 4 * i + 4), i == 0, i == 1)
                    if c == "gv":
                        pe.wait_ge(lev_ready, L * 8 + 1)
                        wait_free(pe, L, "kdT")
                        for q in range(4):
                            mm = pe.transpose(bank[BANK_OF["kdT"]][:, q * P:(q + 1) * P], klev[:, q * P:(q + 1) * P], ident)
                        done(mm, "kdT")
                        for name in ("aq1", "ak1"):
                            wait_drained(pe, L, name)
                        logits(0)
                        logits(1)
                wait_drained(pe, L, "kdT")
                wait_drained(pe, L, "gv1")
                for b, chunks in enumerate(((0, 2), (1,))):
                    wait_free(pe, L, f"U{b}")
                    wait_stands_alone(pe, pe_ticks)
                    for i, c in enumerate(chunks):
                        rows = slice(64 * (c % 2), 64 * (c % 2) + 64)
                        for pair in range(2):
                            for hh in range(2):
                                q = 2 * pair + c // 2
                                h = 2 * pair + hh
                                mm = pe.matmul(bank[BANK_OF[f"U{b}"]][64 * hh:64 * hh + 64, (2 * i + pair) * P:(2 * i + pair + 1) * P],
                                               kdT[rows, q * P + 64 * hh:q * P + 64 * hh + 64],
                                               gv[rows, c // 2, h * P:(h + 1) * P], start=True, stop=True)
                    done(mm, f"U{b}")

                def turn_prob(j):
                    qt, r, m = STEPS[j]
                    name = f"pT{j}"
                    pe.wait_ge(prob_ready, L * 8 + j + 1)
                    wait_free(pe, L, name)
                    nb = qt + 1
                    for i in range(2):
                        for kt in range(nb):
                            q = i * nb + kt
                            mm = pe.transpose(bank[BANK_OF[name]][:, q * P:(q + 1) * P],
                                              prob[:, j % 2, i * nb * P + kt * P:i * nb * P + (kt + 1) * P], ident)
                    done(mm, name)

                def attend(j):
                    qt, r, m = STEPS[j]
                    name = f"oa{j}"
                    wait_drained(pe, L, f"pT{j}")
                    wait_free(pe, L, name)
                    nb = qt + 1
                    for i in range(2):
                        h = 2 * (2 * m + i) + r
                        for kt in range(nb):
                            q = i * nb + kt
                            mm = pe.matmul(bank[BANK_OF[name]][64 * r:64 * r + 64, i * P:(i + 1) * P],
                                           v[:, kt, h * 64:(h + 1) * 64], probT[:, q * P:(q + 1) * P],
                                           start=kt == 0, stop=kt == nb - 1)
                    done(mm, name)

                def level(l):
                    if l:
                        pe.wait_ge(lev_ready, L * 8 + 2 + l)
                    kk, qq = (gkT, gqT) if l == 0 else (klev, qlev)
                    for hh in range(2):
                        name = f"lv{l}{hh}"
                        wait_free(pe, L, name)
                        rows = slice(64 * hh, 64 * hh + 64)
                        for q in range(4):
                            cols, qs = P, qq[rows, q * P:(q + 1) * P]
                            if l:
                                cols, qs = 64, qs.rearrange("p (n w) -> p n w", w=1 << l)[:, :, 1 << l - 1:1 << l]
                            mm = pe.matmul(bank[BANK_OF[name]][:, q * cols:(q + 1) * cols], kk[rows, q * P:(q + 1) * P],
                                           qs, start=True, stop=True)
                        done(mm, name)

                for j in range(8):
                    chunk(MGA + j, f"mg{j}")
                    if j == 0:
                        wait_drained(pe, L, "av1")
                    turn_prob(j)
                    if j < 7:
                        level(j)
                    if j < 6:
                        logits(j + 2)
                    if j >= 1:
                        attend(j - 1)
                def gla_out(t, hh):
                    name = f"go{2 * t + hh}"
                    wait_free(pe, L, name)
                    for pair in range(2):
                        h, q = 2 * pair + hh, 2 * pair + t
                        cols = slice(pair * P, (pair + 1) * P)
                        mm = pe.matmul(bank[BANK_OF[name]][:, cols], amat[:, hh, q * P:(q + 1) * P],
                                       gv[:, t, h * P:(h + 1) * P], start=True, stop=False, skip_group_check=True)
                        for c in range(max(2 * t, 1), 2 * t + 2):
                            at = q * P + 64 * (c % 2)
                            mm = pe.matmul(bank[BANK_OF[name]][64 * (c % 2):64 * (c % 2) + 64, cols],
                                           qdec[64 * hh:64 * hh + 64, at:at + 64], state[64 * hh:64 * hh + 64, c - 1, pair, :],
                                           start=False, stop=True, skip_group_check=True)
                    done(mm, name)

                pe.wait_ge(masked_added, L * 12 + 12)
                wait_drained(pe, L, "U0")
                gla_out(0, 0)
                gla_out(0, 1)
                attend(7)
                gla_out(1, 0)
                gla_out(1, 1)

                def turn_gla():
                    for t in range(2):
                        name = f"gT{t}"
                        wait_drained(pe, L, f"go{2 * t}")
                        wait_drained(pe, L, f"go{2 * t + 1}")
                        if BANK_OF[name] != BANK_OF[f"go{2 * t + 1}"]:
                            wait_free(pe, L, name)
                        for h in range(4):
                            mm = pe.transpose(bank[BANK_OF[name]][:, h * P:(h + 1) * P], go[:, t, h * P:(h + 1) * P], ident)
                        done(mm, name)

                def branch(n, c, xh, xl, i, half):
                    s = operands(L, n + i) if half == 0 else turn(L, n + i)[0]
                    wh, wl = (w[:, s, :].rearrange("p (k n) -> p k n", n=512) for w in (w_hi, w_lo))
                    name = f"{c}{2 * i + half}"
                    wait_free(pe, L, name)
                    for cc in range(2):
                        cs = slice((2 * half + cc) * P, (2 * half + cc + 1) * P)
                        for k in range(4):
                            mm = three(bank[BANK_OF[name]][:, cc * T:(cc + 1) * T], wh[:, k, cs], wl[:, k, cs],
                                       xh[:, k, :], xl[:, k, :], k == 0, k == 3)
                    if half == 0:
                        done(mm, name)
                    else:
                        mm.then_inc(chunk_done[s], 1)

                wait_drained(pe, L, "oa7")
                branch(BRA, "ya", oa_hi, oa_lo, 0, 0)
                branch(BRA, "ya", oa_hi, oa_lo, 0, 1)
                turn_gla()
                branch(BRA, "ya", oa_hi, oa_lo, 1, 0)
                branch(BRA, "ya", oa_hi, oa_lo, 1, 1)
                wait_drained(pe, L, "gT0")
                wait_drained(pe, L, "gT1")
                for i in range(2):
                    for half in range(2):
                        branch(BRB, "yb", obT_hi, obT_lo, i, half)
                for b in range(4):
                    wait_drained(pe, L, LAST_IN_BANK[b])
                for i in range(2):
                    s = operands(L, WOUT + i)
                    pe.wait_ge(merged_lo, L * 4 + i + 1)
                    by_tokens(s, acc, h_hi, h_lo, 1024, range(2 * i, 2 * i + 2), i == 0, False)
                operands(L, WOUT + 2)
                operands(L, WOUT + 3)
                pe.wait_ge(merged_lo, L * 4 + 4)
                for t in range(2):
                    tokens_of(L, [WOUT + 2, WOUT + 3], [(4, 5), (6, 7)], t, lambda k: h_hi[:, k, :], lambda k: h_lo[:, k, :],
                              False, True, turning(L, 2, 0, (6, 7)) if t else {})

            def embed(L):
                s = operands(L, PROJ)
                pe.wait_ge(pT_lo, L + 1)
                wh, wl = (w[:, s, :].rearrange("p (k n) -> p k n", n=1024) for w in (w_hi, w_lo))
                for t in range(2):
                    pe.wait_ge(x_ready, L * 16 + 12 + 2 * t + 2)
                    for c in range(2):
                        for k in range(2):
                            mm = three(bank[2 * t + c][:, :], pT_hi_[:, k, t * P:(t + 1) * P], pT_lo_[:, k, t * P:(t + 1) * P],
                                       wh[:, k, c * 512:(c + 1) * 512], wl[:, k, c * 512:(c + 1) * 512], k == 0, k == 1)
                    if t == 0:
                        mm.then_inc(proj_half, 1)
                        for half in range(2):
                            turn_half(L, 3, 0, half)
                    else:
                        mm.then_inc(chunk_done[s], 1)
                h = (lambda k: h_hi[:, k, :], lambda k: h_lo[:, k, :])
                operands(L, PGATE)
                pe.wait_ge(proj_out, L * 4 + 2)
                pe.wait_ge(h_lo_ready, L * 16 + 12 + 2)
                tokens_of(L, [PGATE], [(0, 1)], 0, *h, True, False, turning(L, 3, 1, (1, 3)))
                operands(L, PGATE + 1)
                tokens_of(L, [PGATE + 1], [(2, 3)], 0, *h, False, False)
                pe.wait_ge(proj_out, L * 4 + 4)
                pe.wait_ge(h_lo_ready, L * 16 + 12 + 4)
                tokens_of(L, [PGATE, PGATE + 1], [(0, 1), (2, 3)], 1, *h, True, False)
                operands(L, PGATE + 2)
                tokens_of(L, [PGATE + 2], [(4, 5)], 0, *h, False, False)
                operands(L, PGATE + 3)
                tokens_of(L, [PGATE + 3], [(6, 7)], 0, *h, False, True)
                tokens_of(L, [PGATE + 2, PGATE + 3], [(4, 5), (6, 7)], 1, *h, False, True, turning(L, 4, 0, (7,)))
                turn_half(L, 4, 0, 1)

            start_counts(pe, chunk_done)
            pe.wait_ge(const_landed, 16)
            for half in range(2):
                turn_half(0, 0, 0, half)
            with pe.Fori(0, L_N) as L:
                ffn(L, FF1, 0)
                mix(L)
                ffn(L, FF2, 1)
                embed(L)

        @block.scalar
        def _(act):
            steps = [0]

            def step(L, ins):
                ins.then_inc(scalar_step, 1)
                steps[0] += 1
                act.wait_ge(scalar_step, L * SCALAR_STEPS + steps[0])

            def split(L, n, g=0):
                s, t = turn(L, n, g)
                act.wait_ge(landed[s], t * 16)
                if n == SMALL:
                    act.wait_ge(extra_landed, (L + 1) * 32)
                act.wait_ge(chunk_done[s], t - 1 + START)
                act.activation(w_hi[:, s, :], raw[:, s, :], ACT.Copy).then_inc(hi_ready[s], 1)

            def chunk_products(L, n, g=0):
                s, t = turn(L, n, g)
                act.wait_ge(chunk_done[s], t + START)

            def squares(L, k, t):
                for c in range(2):
                    act.wait_ge(x_ready, L * 16 + 4 * k + 2 * t + c + 1)
                    cols = slice(c * 512, (c + 1) * 512)
                    act.activation(xn[:, t, cols], x[:, t, cols], ACT.Square, accum_out=ssq[:, 2 * t + c:2 * t + c + 1]
                                   ).then_inc(ssq_done, 1)

            def round_h(L, k, t):
                for h in range(2):
                    act.wait_ge(turned[h], L * 8 + 2 * k + t + 1)
                    act.activation(h_hi[:, 4 * h:4 * h + 4, t * P:(t + 1) * P],
                                   bank[6 + h][:, :].rearrange("p (k n) -> p k n", n=P), ACT.Copy).then_inc(h_hi_ready, 1)

            def norm(L, k, second):
                if k:
                    squares(L, k, 0)
                    split(L, second)
                    round_h(L, k, 0)
                squares(L, k, 1)
                split(L, second + 1)
                round_h(L, k, 1)

            def ffn(L, off, f):
                F = L * 22 + f * 11

                def silu_gate(n, g, group):
                    chunk_products(L, n, g)
                    act.wait_ge(hidden_done, F + group + START)
                    act.activation(silu[:, :], bank[4][:, :], ACT.Silu).then_inc(silu_done, 1)

                def round_hidden(group, par):
                    act.wait_ge(hidden_done, F + group + 1 + START)
                    act.activation(small_hi[:, par, :], hidden[:, par, :], ACT.Copy).then_inc(hidden_hi, 1)

                def round_turned_hidden():
                    act.wait_ge(hidden_turned, L * 2 + f + 1)
                    act.activation(small_hi[:, 0, :], bank[6][:, :], ACT.Copy).then_inc(hidden_hi, 1)

                silu_gate(off, 0, 0)
                split(L, off + 3)
                round_turned_hidden()
                split(L, off + 4)
                silu_gate(off + 2, 0, 1)
                split(L, off + 5)
                round_hidden(1, 1)
                split(L, off + 6)
                split(L, off + 7)
                with act.Fori(0, 4) as i:
                    for j in range(2):
                        g = i * 2 + (j + 2)
                        silu_gate(off + 5 + 3 * j, i * 2, g)
                        split(L, off + 8 + 3 * j, i * 2)
                        chunk_products(L, off + 4 + 3 * j, i * 2)
                        round_hidden(g, j)
                        split(L, off + 9 + 3 * j, i * 2)
                        split(L, off + 10 + 3 * j, i * 2)
                silu_gate(off + 29, 0, 10)
                split(L, off + 32)
                chunk_products(L, off + 28)
                round_hidden(10, 0)
                split(L, off + 33)
                if f == 1:
                    act.wait_ge(p_turned, L + 1)
                    act.activation(small_hi[:, 2, :], bank[6][:, :], ACT.Copy).then_inc(pT_hi, 1)

            def take(L, job, dst, func=ACT.Copy, scale=1.0, n=512):
                act.activation(dst, bank[BANK_OF[job]][:, 0:n], func, scale=scale).then_inc(drained[BANK_OF[job]], 1)

            def flat(t):
                return t.rearrange("p a b -> p (a b)")

            def mix(L):
                split(L, MIX + 3)
                chunk_products(L, AV + 1)
                split(L, MIX + 4)
                for t in range(2):
                    take(L, f"av{t}", v[:, t, :])
                chunk_products(L, SMALL)
                take(L, "small", flat(ikT[:, :, :]))
                split(L, MIX + 5)
                for i in range(2):
                    chunk_products(L, IQ + i)
                    take(L, f"iq{i}", flat(iqT[:, 2 * i:2 * i + 2, :]))
                    split(L, MIX + 6 + i)
                wait_filled(act, L, "wi")
                act.activation(wi[:, :, :], bank[BANK_OF["wi"]][:, 0:2 * P].rearrange("p (t c) -> p t c", t=2)[:, :, 0:8], ACT.Copy,
                               scale=float(64 ** -0.5 * 8 ** -0.5)).then_inc(drained[BANK_OF["wi"]], 1)
                for j in range(8):
                    nk = P * (STEPS[j][0] + 1)
                    wait_filled(act, L, f"sc{j}")
                    if j >= 2:
                        act.wait_ge(scores_added, L * 8 + j - 1)
                    take(L, f"sc{j}", relu[:, j % 2, 0:2 * nk], ACT.Relu, n=2 * nk)
                chunk_products(L, GQ)
                take(L, "gq", gqT[:, :], scale=0.125)
                split(L, MIX + 8)
                chunk_products(L, GK)
                take(L, "gk", gkT[:, :])
                split(L, MIX + 9)
                wait_filled(act, L, "glog")
                act.wait_ge(layer_landed, (L + 1) * 64)
                zb = bank[BANK_OF["glog"]]
                act.activation(zg[:, 0:T], zb[:, 0:T], ACT.Identity, bias=gbias[:, 0:1])
                act.activation(zg[:, T:2 * T], zb[:, T:2 * T], ACT.Identity, bias=gbias[:, 1:2]).then_inc(drained[BANK_OF["glog"]], 1)
                wait_drained(act, L, "glog")
                step(L, act.activation(decay_abs, zg[:, :], ACT.Abs))
                step(L, act.activation(decay_ln, decay_abs, ACT.Exp, scale=-1.0))
                act.activation(decay_ln, decay_ln, ACT.Ln, bias=1.0).then_inc(gla_exp, 1)
                chunk_products(L, AQ)
                take(L, "aq0", flat(qT[:, 0:2, :]))
                split(L, MIX + 10)
                chunk_products(L, AQ + 1)
                take(L, "aq1", flat(qT[:, 2:4, :]))
                split(L, MIX + 11)
                act.wait_ge(gla_scan, L + 1)
                act.activation(qdec[:, :], bcum[:, :], ACT.Exp, scale=1.0 / 16)
                act.activation(dec[:, :], bcum[:, 63:512:64], ACT.Exp, scale=1.0 / 16).then_inc(gla_exp, 1)
                act.wait_ge(lev_dist, L * 7 + 1)
                act.activation(lev[:, :], dist[:, :], ACT.Exp, scale=-1.0 / 16).then_inc(gla_exp, 1)
                for i in range(2):
                    chunk_products(L, AK + i)
                    take(L, f"ak{i}", flat(kT[:, 2 * i:2 * i + 2, :]))
                    split(L, MIX + 12 + i)
                split(L, MIX + 14)
                chunk_products(L, GV + 1)
                for t in range(2):
                    take(L, f"gv{t}", gv[:, t, :])
                split(L, MIX + 15)
                wait_filled(act, L, "kdT")
                take(L, "kdT", kdT[:, :])
                split(L, MIX + 16)
                def exps(j):
                    nk = P * (STEPS[j][0] + 1)
                    act.wait_ge(logit_ready, L * 8 + j + 1)
                    if j >= 2:
                        wait_filled(act, L, f"pT{j - 2}")
                    for i in range(2):
                        ins = act.activation(prob[:, j % 2, i * nk:(i + 1) * nk], relu[:, j % 2, i * nk:(i + 1) * nk], ACT.Exp,
                                             scale=0.125, bias=nmx[:, j % 2, i:i + 1], accum_out=psums[:, j % 2, i:i + 1])
                    ins.then_inc(prob_exp, 1)

                exps(0)
                chunk_products(L, GR + 1)
                for t in range(2):
                    act.activation(gsilu[:, t, :], bank[BANK_OF[f"gr{t}"]][:, :], ACT.Tanh, scale=0.5).then_inc(gr_tanh, 1)
                exps(1)
                split(L, MIX + 17)

                def round_oa(j):
                    qt, r, m = STEPS[j]
                    rows = slice(64 * r, 64 * r + 64)
                    wait_filled(act, L, f"oa{j}")
                    act.activation(oa_hi[rows, 2 * m:2 * m + 2, qt * P:(qt + 1) * P],
                                   bank[BANK_OF[f"oa{j}"]][rows, 0:2 * P].rearrange("p (i q) -> p i q", i=2),
                                   ACT.Copy).then_inc(oa_hi_ready, 1)

                for j in range(8):
                    nk = P * (STEPS[j][0] + 1)
                    chunk_products(L, MGA + j)
                    gate = gate_a[:, 2 * j:2 * j + 2, :] if j < 4 else gate_b[:, 2 * j - 8:2 * j - 6, :]
                    take(L, f"mg{j}", flat(gate), ACT.Tanh, scale=0.5)
                    if j < 6:
                        act.wait_ge(lev_dist, L * 7 + 2 + j)
                        act.wait_ge(lev_ready, L * 8 + 2 + j)
                        step(L, act.activation(lev[:, :], dist[:, :], ACT.Abs))
                        act.activation(lev[:, :], lev[:, :], ACT.Exp, scale=-1.0 / 16).then_inc(gla_exp, 1)
                    if 0 < j < 7:
                        exps(j + 1)
                    split(L, MGA + j + 3)
                    wait_filled(act, L, f"pT{j}")
                    if j >= 1:
                        wait_filled(act, L, f"oa{j - 1}")
                    take(L, f"pT{j}", probT[:, 0:2 * nk], n=2 * nk)
                    if j >= 1:
                        round_oa(j - 1)
                for q in range(4):
                    t, hh = q // 2, q % 2
                    if q == 2:
                        round_oa(7)
                    wait_filled(act, L, f"go{q}")
                    for pair in range(2):
                        h = 2 * pair + hh
                        ins = act.activation(go[:, t, h * P:(h + 1) * P], bank[BANK_OF[f"go{q}"]][:, pair * P:(pair + 1) * P],
                                             ACT.Square, accum_out=gss[:, 4 * t + h:4 * t + h + 1])
                    ins.then_inc(gss_done, 1)
                for t in range(2):
                    wait_filled(act, L, f"gT{t}")
                    act.activation(obT_hi[:, :, t * P:(t + 1) * P], bank[BANK_OF[f"gT{t}"]][:, :].rearrange("p (h t) -> p h t", h=4),
                                   ACT.Copy).then_inc(gT_hi_ready, 1)
                split(L, BRB + 1)
                split(L, WOUT)
                split(L, WOUT + 1)
                for i in range(4):
                    act.wait_ge(merged, L * 4 + i + 1)
                    act.activation(h_hi[:, 2 * i:2 * i + 2, :], gate_b[:, 2 * i:2 * i + 2, :], ACT.Copy).then_inc(merged_hi, 1)
                    if i == 1:
                        split(L, WOUT + 2)
                split(L, WOUT + 3)
                split(L, FF2)

            def embed(L, last):
                def take_projection(t):
                    for q in (2 * t, 2 * t + 1):
                        act.activation(proj[:, t, (q % 2) * 512:(q % 2 + 1) * 512], bank[q][:, :], ACT.Copy, scale=0.5
                                       ).then_inc(proj_out, 1)

                squares(L, 3, 0)
                split(L, PGATE)
                act.wait_ge(proj_half, L + 1)
                take_projection(0)
                round_h(L, 3, 0)
                squares(L, 3, 1)
                split(L, PGATE + 1)
                chunk_products(L, PROJ)
                take_projection(1)
                round_h(L, 3, 1)
                split(L, PGATE + 2)
                split(L, PGATE + 3)
                if not last:
                    split(L, CHUNKS)
                act.wait_ge(acc_ready, L * 4 + 4)
                for q in range(4):
                    if q == 2:
                        squares(L, 4, 0)
                        if not last:
                            split(L, CHUNKS + 1)
                        chunk_products(L, PGATE + 3)
                    act.activation(xn[:, q // 2, (q % 2) * 512:(q % 2 + 1) * 512], bank[q][:, :], ACT.Tanh, scale=0.5
                                   ).then_inc(pgate_out, 1)
                if not last:
                    round_h(L, 4, 0)

            start_counts(act, [silu_done] + drained)
            def layer(L, last):
                norm(L, 0, 1)
                ffn(L, FF1, 0)
                norm(L, 1, MIX + 1)
                mix(L)
                norm(L, 2, FF2 + 1)
                ffn(L, FF2, 1)
                embed(L, last)
                assert steps[0] == SCALAR_STEPS, steps
                steps[0] = 0

            squares(0, 0, 0)
            split(0, 0)
            round_h(0, 0, 0)
            split(0, 1)
            with act.Fori(0, L_N - 1) as L:
                layer(L, False)
            layer(L_N - 1, True)
            squares(L_N, 0, 1)

        @block.gpsimd
        def _(pool):
            steps = [0]

            def step(L, ins):
                ins.then_inc(pool_step, 1)
                steps[0] += 1
                pool.wait_ge(pool_step, L * POOL_STEPS + steps[0])

            def root(L, out_, done):
                pool.tensor_tensor(out_, out_, half_neg[:, 0:out_.shape[1]], ALU.pow).then_inc(done, 1)

            def norm(L, k):
                for t in range(2):
                    at = L * 16 + 4 * k + 2 * t
                    pool.wait_ge(ssq_done, at + 1)
                    wait_stands_alone(pool, pool_ticks)
                    step(L, pool.tensor_scalar(mean[:, t:t + 1], ssq[:, 2 * t:2 * t + 1], 1.0 / D, EPS, ALU.mult, ALU.add))
                    pool.wait_ge(ssq_done, at + 2)
                    wait_stands_alone(pool, pool_ticks)
                    step(L, pool.tensor_scalar(rstd[:, t:t + 1], ssq[:, 2 * t + 1:2 * t + 2], 1.0 / D, mean[:, t:t + 1],
                                               ALU.mult, ALU.add))
                    root(L, rstd[:, t:t + 1], rstd_done)

            pool.memset(w2[:, :], 0.0).then_inc(w2_zeroed, 1)
            pool.memset(half_neg[:, :], -0.5).then_inc(half_ready, 1)
            pool.wait_ge(half_ready, 1)
            with pool.Fori(0, L_N) as L:
                norm(L, 0)
                norm(L, 1)
                pool.wait_ge(gla_exp, L * 9 + 3)
                wait_drained(pool, L, "gk")
                pool.tensor_tensor(klev[:, :], gkT[:, :], lev[:, :], ALU.mult).then_inc(lev_ready, 1)
                pool.tensor_tensor(qdec[:, :], gqT[:, :], qdec[:, :], ALU.mult).then_inc(lev_ready, 1)
                for j in range(7):
                    if j < 6:
                        pool.wait_ge(gla_exp, L * 9 + 4 + j)
                        wait_filled(pool, L, f"lv{j}1" if j else "kdT")
                        pool.tensor_tensor(klev[:, :], gkT[:, :], lev[:, :], ALU.mult)
                        pool.tensor_tensor(qlev[:, :], gqT[:, :], lev[:, :], ALU.mult).then_inc(lev_ready, 1)
                    if j:
                        for hh in range(2):
                            wait_drained(pool, L, f"lv{j}{hh}")
                            if j >= 2:
                                pool.wait_ge(masked_added, L * 12 + 2 * (j - 2) + hh + 1)
                            at = amat[:, hh, :].rearrange("p (n w) -> p n w", w=1 << j)[:, :, 1 << j - 1:1 << j]
                            pool.tensor_tensor(at, at, masked[:, hh, 0:256].rearrange("p (n w) -> p n w", w=1 << j - 1), ALU.add
                                               ).then_inc(masked_added, 1)
                for t in range(2):
                    pool.wait_ge(gss_done, L * 4 + 2 * t + 2)
                    wait_stands_alone(pool, pool_ticks)
                    gr = grstd[:, 4 * t:4 * t + 4]
                    step(L, pool.tensor_scalar(gr, gss[:, 4 * t:4 * t + 4], 1.0 / P, EPS, ALU.mult, ALU.add))
                    root(L, gr, grstd_done)
                norm(L, 2)
                norm(L, 3)
            assert steps[0] == POOL_STEPS, steps
            steps[0] = 0
            norm(L_N, 0)

        @block.vector
        def _(dve):
            steps = [0]

            def step(L, ins):
                ins.then_inc(vector_step, 1)
                steps[0] += 1
                dve.wait_ge(vector_step, L * VECTOR_STEPS + steps[0])

            def split(L, n, g=0):
                s, t = turn(L, n, g)
                dve.wait_ge(hi_ready[s], t)
                dve.tensor_tensor(w_lo[:, s, :], raw[:, s, :], w_hi[:, s, :].bitcast(F32), ALU.subtract).then_inc(lo_ready[s], 1)

            def chunk_products(L, n, g=0):
                s, t = turn(L, n, g)
                dve.wait_ge(chunk_done[s], t + START)

            def scaled_tile(L, k, t):
                dve.wait_ge(rstd_done, L * 8 + 2 * k + t + 1)
                for c in range(2):
                    cols = slice(c * 512, (c + 1) * 512)
                    dve.scalar_tensor_tensor(out=xn[:, t, cols], in0=x[:, t, cols], scalar=rstd[:, t:t + 1], in1=gain[:, cols],
                                             op0=ALU.mult, op1=ALU.mult).then_inc(xn_ready, 1)

            def rest_h(L, k, t):
                for h in range(2):
                    dve.wait_ge(h_hi_ready, L * 16 + 4 * k + 2 * t + h + 1)
                    hi = h_hi[:, 4 * h:4 * h + 4, t * P:(t + 1) * P]
                    dve.tensor_tensor(h_lo[:, 4 * h:4 * h + 4, t * P:(t + 1) * P],
                                      bank[6 + h][:, :].rearrange("p (k n) -> p k n", n=P), hi.bitcast(F32),
                                      ALU.subtract).then_inc(h_lo_ready, 1)

            def norm(L, k, second, update):
                dve.wait_ge(gain_landed, (L * 4 + k + 1) * 16)
                if k:
                    update(0)
                    scaled_tile(L, k, 0)
                if k == 3:
                    update(1)
                    split(L, second)
                if k:
                    rest_h(L, k, 0)
                if 0 < k < 3:
                    update(1)
                if k < 3:
                    split(L, second)
                scaled_tile(L, k, 1)
                if k == 3:
                    split(L, second + 1)
                rest_h(L, k, 1)
                if k < 3:
                    split(L, second + 1)

            def add_half(L, n, phase):
                def update(t):
                    if t == 0:
                        dve.wait_ge(acc_ready, L * 4 + phase)
                    else:
                        chunk_products(L, n)
                    for q in (2 * t, 2 * t + 1):
                        xs = x[:, t, (q % 2) * 512:(q % 2 + 1) * 512]
                        dve.scalar_tensor_tensor(out=xs, in0=bank[q][:, :], scalar=0.5, in1=xs, op0=ALU.mult, op1=ALU.add
                                                 ).then_inc(x_ready, 1)
                return update

            def ffn(L, off, f):
                F = L * 22 + f * 11

                def gated(n, g, group, par):
                    chunk_products(L, n, g)
                    dve.wait_ge(silu_done, F + group + 1 + START)
                    dve.tensor_tensor(hidden[:, par, :], silu[:, :], bank[5][:, :], ALU.mult).then_inc(hidden_done, 1)

                def turned_hidden_rest():
                    dve.wait_ge(hidden_hi, F + 1)
                    dve.tensor_tensor(small_lo[:, 0, :], bank[6][:, :], small_hi[:, 0, :].bitcast(F32),
                                      ALU.subtract).then_inc(hidden_lo, 1)

                def hidden_rest(group, par):
                    dve.wait_ge(hidden_hi, F + group + 1)
                    dve.tensor_tensor(small_lo[:, par, :], hidden[:, par, :], small_hi[:, par, :].bitcast(F32),
                                      ALU.subtract).then_inc(hidden_lo, 1)

                gated(off + 1, 0, 0, 0)
                split(L, off + 3)
                turned_hidden_rest()
                split(L, off + 4)
                split(L, off + 5)
                gated(off + 3, 0, 1, 1)
                hidden_rest(1, 1)
                split(L, off + 6)
                split(L, off + 7)
                with dve.Fori(0, 4) as i:
                    for j in range(2):
                        g = i * 2 + (j + 2)
                        split(L, off + 8 + 3 * j, i * 2)
                        dve.wait_ge(hidden_lo, F + g - 1)
                        gated(off + 6 + 3 * j, i * 2, g, j)
                        hidden_rest(g, j)
                        split(L, off + 9 + 3 * j, i * 2)
                        split(L, off + 10 + 3 * j, i * 2)
                dve.wait_ge(hidden_lo, F + 9)
                split(L, off + 32)
                gated(off + 30, 0, 10, 0)
                hidden_rest(10, 0)
                split(L, off + 33)
                if f == 1:
                    dve.wait_ge(pT_hi, L + 1)
                    dve.tensor_tensor(small_lo[:, 2, :], bank[6][:, :], small_hi[:, 2, :].bitcast(F32), ALU.subtract).then_inc(pT_lo, 1)

            def top_k(L, qt):
                nk = P * (qt + 1)
                sc = score[:, qt, 0:nk]
                step(L, dve.memset(score[0:64, qt, nk - 64:nk], INADMISSIBLE))
                for _ in range(8):
                    wait_stands_alone(dve, dve_ticks)
                    step(L, dve.max(top8[:, :], sc))
                    wait_stands_alone(dve, dve_ticks)
                    step(L, dve.match_replace(sc, top8[:, :], sc, REPLACED))
                dve.tensor_scalar(selbias[:, qt, 0:nk], sc, -3.0e38, FAR, ALU.is_ge, ALU.mult).then_inc(selected, 1)

            def mix(L):
                split(L, MIX + 3)
                split(L, MIX + 4)
                split(L, MIX + 5)
                split(L, MIX + 6)
                split(L, MIX + 7)
                wait_drained(dve, L, "wi")
                for j in range(8):
                    qt, r, m = STEPS[j]
                    nk = P * (qt + 1)
                    wait_drained(dve, L, f"sc{j}")
                    for i in range(2):
                        h = 2 * (2 * m + i) + r
                        rl = relu[:, j % 2, i * nk:(i + 1) * nk]
                        sc = score[:, qt, 0:nk]
                        if j % 4 == 0 and i == 0:
                            ins = dve.tensor_scalar(sc, rl, wi[:, qt, h:h + 1], None, ALU.mult)
                        else:
                            ins = dve.scalar_tensor_tensor(out=sc, in0=rl, scalar=wi[:, qt, h:h + 1], in1=sc,
                                                           op0=ALU.mult, op1=ALU.add)
                        if i == 0:
                            step(L, ins)
                        else:
                            ins.then_inc(scores_added, 1)
                            dve.wait_ge(scores_added, L * 8 + j + 1)
                split(L, MIX + 8)
                top_k(L, 0)
                split(L, MIX + 9)
                dve.wait_ge(gla_exp, L * 9 + 1)
                step(L, dve.scalar_tensor_tensor(out=dist[:, :], in0=zg[:, :], scalar=0.0, in1=decay_ln,
                                                 op0=ALU.min, op1=ALU.subtract))
                dve.tensor_tensor_scan(bcum[:, :], reset, dist[:, :], 0.0, ALU.mult, ALU.add).then_inc(gla_scan, 1)
                split(L, MIX + 10)
                dve.wait_ge(gla_scan, L + 1)

                def distance(width, at):
                    b = bcum[:, :].rearrange("p (n w) -> p n w", w=width)
                    ref = b[:, :, at:at + 1].to_broadcast([P, 512 // width, width])
                    dve.tensor_tensor(dist[:, :].rearrange("p (n w) -> p n w", w=width), b, ref, ALU.subtract).then_inc(lev_dist, 1)

                distance(64, 63)
                split(L, MIX + 11)
                top_k(L, 1)
                split(L, MIX + 12)
                split(L, MIX + 13)
                split(L, MIX + 14)
                split(L, MIX + 15)
                split(L, MIX + 16)

                def mask_logits(j):
                    qt = STEPS[j][0]
                    nk = P * (qt + 1)
                    name = f"lg{j}"
                    wait_filled(dve, L, name)
                    if j >= 2:
                        dve.wait_ge(prob_exp, L * 8 + j - 1)
                    lm = relu[:, j % 2, 0:2 * nk].rearrange("p (i k) -> p i k", i=2)
                    sel = selbias[:, qt:qt + 1, 0:nk].to_broadcast([P, 2, nk])
                    dve.tensor_tensor(lm, bank[BANK_OF[name]][:, 0:2 * nk].rearrange("p (i k) -> p i k", i=2), sel, ALU.add
                                      ).then_inc(drained[BANK_OF[name]], 1)
                    wait_drained(dve, L, name)
                    step(L, dve.tensor_reduce(mx[:, j % 2, :], lm, AX_X, ALU.max))
                    dve.tensor_scalar(nmx[:, j % 2, :], mx[:, j % 2, :], -0.125, None, ALU.mult).then_inc(logit_ready, 1)

                def normalise(j):
                    nk = P * (STEPS[j][0] + 1)
                    dve.wait_ge(prob_exp, L * 8 + j + 1)
                    step(L, dve.reciprocal(rsum[:, j % 2, :], psums[:, j % 2, :]))
                    for i in range(2):
                        pr = prob[:, j % 2, i * nk:(i + 1) * nk]
                        ins = dve.tensor_scalar(pr, pr, rsum[:, j % 2, i:i + 1], None, ALU.mult)
                    ins.then_inc(prob_ready, 1)

                dve.wait_ge(selected, L * 2 + 2)
                mask_logits(0)
                mask_logits(1)
                for t in range(2):
                    name = f"gr{t}"
                    dve.wait_ge(gr_tanh, L * 2 + t + 1)
                    dve.scalar_tensor_tensor(out=gsilu[:, t, :], in0=gsilu[:, t, :], scalar=1.0, in1=bank[BANK_OF[name]][:, :],
                                             op0=ALU.add, op1=ALU.mult).then_inc(drained[BANK_OF[name]], 1)
                for t in range(2):
                    wait_drained(dve, L, f"gr{t}")
                    g = gsilu[:, t, :].rearrange("p (h e) -> p h e", h=4)
                    gn = gnorm[:, :].unsqueeze(1).to_broadcast([P, 4, P])
                    dve.scalar_tensor_tensor(out=g, in0=g, scalar=0.5, in1=gn, op0=ALU.mult, op1=ALU.mult).then_inc(gsilu_done, 1)
                normalise(0)
                normalise(1)

                u0 = bank[BANK_OF["U0"]][:, :].rearrange("p (c h e) -> p c h e", c=2, h=2)
                u1 = bank[BANK_OF["U1"]][:, 0:256].rearrange("p (h e) -> p h e", h=2)
                wait_filled(dve, L, "U0")
                wait_filled(dve, L, "U1")
                step(L, dve.tensor_copy(state[:, 0, :, :], u0[:, 0, :, :]))
                for c, u, job in [(1, u1, "U1"), (2, u0[:, 1, :, :], "U0")]:
                    for pair in range(2):
                        ins = dve.scalar_tensor_tensor(out=state[:, c, pair, :], in0=state[:, c - 1, pair, :],
                                                       scalar=dec[:, 4 * pair + c:4 * pair + c + 1], in1=u[:, pair, :],
                                                       op0=ALU.mult, op1=ALU.add)
                    ins.then_inc(drained[BANK_OF[job]], 1)
                    wait_drained(dve, L, job)

                def rest_oa(j):
                    qt, r, m = STEPS[j]
                    rows = slice(64 * r, 64 * r + 64)
                    dve.wait_ge(oa_hi_ready, L * 8 + j + 1)
                    at = (rows, slice(2 * m, 2 * m + 2), slice(qt * P, (qt + 1) * P))
                    dve.tensor_tensor(oa_lo[at], bank[BANK_OF[f"oa{j}"]][rows, 0:2 * P].rearrange("p (i q) -> p i q", i=2),
                                      oa_hi[at].bitcast(F32), ALU.subtract).then_inc(drained[BANK_OF[f"oa{j}"]], 1)

                dve.wait_ge(gla_exp, L * 9 + 3)
                distance(2, 0)
                split(L, MIX + 17)
                for j in range(8):
                    if j < 5:
                        dve.wait_ge(gla_exp, L * 9 + 4 + j)
                        distance(4 << j, (2 << j) - 1)
                    split(L, MGA + j + 3)
                    if 0 < j < 7:
                        normalise(j + 1)
                    if j < 7:
                        for hh in range(2):
                            name = f"lv{j}{hh}"
                            wait_filled(dve, L, name)
                            if j >= 2:
                                dve.wait_ge(masked_added, L * 12 + 2 * (j - 2) + hh + 1)
                            if j == 0:
                                dst, mask, w = amat[:, hh, :], ident, P
                            else:
                                dst, mask, w = masked[:, hh, 0:256], consts[:, P + 64 * (j - 1):P + 64 * j], 64
                            dve.tensor_tensor(dst.rearrange("p (q t) -> p q t", q=4),
                                              bank[BANK_OF[name]][:, 0:4 * w].rearrange("p (q t) -> p q t", q=4),
                                              mask.unsqueeze(1).to_broadcast([P, 4, w]), ALU.mult
                                              ).then_inc(drained[BANK_OF[name]], 1)
                    if j >= 1:
                        rest_oa(j - 1)
                    if j < 6:
                        mask_logits(j + 2)
                rest_oa(7)
                dve.wait_ge(gsilu_done, L * 2 + 2)
                for t in range(2):
                    dve.wait_ge(grstd_done, L * 2 + t + 1)
                    for hh in range(2):
                        name = f"go{2 * t + hh}"
                        for pair in range(2):
                            h = 2 * pair + hh
                            ins = dve.scalar_tensor_tensor(out=go[:, t, h * P:(h + 1) * P],
                                                           in0=bank[BANK_OF[name]][:, pair * P:(pair + 1) * P],
                                                           scalar=grstd[:, 4 * t + h:4 * t + h + 1],
                                                           in1=gsilu[:, t, h * P:(h + 1) * P], op0=ALU.mult, op1=ALU.mult)
                        ins.then_inc(drained[BANK_OF[name]], 1)

                def gate_branch(c, i, gate):
                    name = f"{c}{i}"
                    if i % 2:
                        chunk_products(L, (BRA if c == "ya" else BRB) + i // 2)
                    else:
                        wait_filled(dve, L, name)
                    g = flat_(gate[:, 2 * i:2 * i + 2, :])
                    dve.scalar_tensor_tensor(out=g, in0=g, scalar=1.0, in1=bank[BANK_OF[name]][:, :],
                                             op0=ALU.add, op1=ALU.mult).then_inc(drained[BANK_OF[name]], 1)

                def flat_(t):
                    return t.rearrange("p a b -> p (a b)")

                gate_branch("ya", 0, gate_a)
                gate_branch("ya", 1, gate_a)
                for t in range(2):
                    dve.wait_ge(gT_hi_ready, L * 2 + t + 1)
                    name = f"gT{t}"
                    dve.tensor_tensor(obT_lo[:, :, t * P:(t + 1) * P], bank[BANK_OF[name]][:, :].rearrange("p (h t) -> p h t", h=4),
                                      obT_hi[:, :, t * P:(t + 1) * P].bitcast(F32), ALU.subtract
                                      ).then_inc(drained[BANK_OF[name]], 1)
                split(L, BRB + 1)
                gate_branch("ya", 2, gate_a)
                gate_branch("ya", 3, gate_a)
                split(L, WOUT)

                for i in range(4):
                    gate_branch("yb", i, gate_b)
                    wait_drained(dve, L, f"yb{i}")
                    ga, gb = gate_a[:, 2 * i:2 * i + 2, :], gate_b[:, 2 * i:2 * i + 2, :]
                    dve.tensor_tensor(flat_(gb), flat_(ga), flat_(gb), ALU.add).then_inc(merged, 1)
                    if i == 1:
                        split(L, WOUT + 1)
                    if i % 2:
                        for u in (i - 1, i):
                            dve.wait_ge(merged_hi, L * 4 + u + 1)
                            dve.tensor_tensor(h_lo[:, 2 * u:2 * u + 2, :], gate_b[:, 2 * u:2 * u + 2, :],
                                              h_hi[:, 2 * u:2 * u + 2, :].bitcast(F32), ALU.subtract).then_inc(merged_lo, 1)
                split(L, WOUT + 2)
                split(L, WOUT + 3)
                split(L, FF2)

            def embed(L, last):
                norm(L, 3, PGATE, add_half(L, FF2 + 3 * N_FF - 1, 3))
                split(L, PGATE + 2)
                split(L, PGATE + 3)
                if not last:
                    split(L, CHUNKS)
                for q in range(4):
                    dve.wait_ge(pgate_out, L * 4 + q + 1)
                    cols = slice((q % 2) * 512, (q % 2 + 1) * 512)
                    g = xn[:, q // 2, cols]
                    step(L, dve.scalar_tensor_tensor(out=g, in0=g, scalar=1.0, in1=proj[:, q // 2, cols], op0=ALU.add, op1=ALU.mult))
                    dve.tensor_tensor(x[:, q // 2, cols], x[:, q // 2, cols], g, ALU.add).then_inc(x_ready, 1)
                    if q == 1:
                        dve.wait_ge(gain_landed, (L * 4 + 5) * 16)
                        scaled_tile(L, 4, 0)
                if not last:
                    rest_h(L, 4, 0)

            start_counts(dve, lo_ready + [hidden_done, xn_ready])
            def layer(L, last):
                norm(L, 0, 1, None)
                ffn(L, FF1, 0)
                norm(L, 1, MIX + 1, add_half(L, MIX - 1, 1))
                mix(L)
                norm(L, 2, FF2 + 1, add_half(L, FF2 - 1, 2))
                ffn(L, FF2, 1)
                embed(L, last)
                assert steps[0] == VECTOR_STEPS, steps
                steps[0] = 0

            dve.wait_ge(x_landed[0], 16)
            dve.sem_inc(x_ready, 2)
            dve.wait_ge(gain_landed, 16)
            scaled_tile(0, 0, 0)
            split(0, 0)
            rest_h(0, 0, 0)
            dve.wait_ge(x_landed[1], 16)
            dve.sem_inc(x_ready, 2)
            with dve.Fori(0, L_N - 1) as L:
                layer(L, False)
            layer(L_N - 1, True)
            dve.wait_ge(gain_landed, (L_N * 4 + 1) * 16)
            scaled_tile(L_N, 0, 1)


def constants():
    s, t = np.arange(P)[:, None], np.arange(P)[None, :]
    parts = [s == t]
    for level in range(1, 7):
        b = 1 << level
        parts.append(((s // b == t // b) & (s % b < b // 2))[:, np.arange(P) % b >= b // 2])
    parts.append(np.broadcast_to(np.arange(512) % 64 != 0, (P, 512)))
    return np.ascontiguousarray(np.concatenate(parts, axis=1).astype(np.float32))


INPUTS = ["x", "p", "w_in", "gla_gate_w2", "gla_gate_b", "gla_norm", "w_branch_a", "w_branch_b", "w_out", "norm_ff1",
          "norm_mix", "norm_ff2", "norm_ple", "ff1_w_gate", "ff1_w_up", "ff1_w_down", "ff2_w_gate", "ff2_w_up",
          "ff2_w_down", "ple_w_proj", "ple_w_gate", "norm_final"]


def kernel(**inputs):
    import concourse.bacc as bacc
    from concourse.bass_utils import run_bass_kernel_spmd

    nc = bacc.Bacc("TRN2", target_bir_lowering=False, num_devices=1)
    arrays = {name: np.ascontiguousarray(inputs[name]) for name in INPUTS}
    arrays["consts"] = constants()
    args = {name: nc.dram_tensor(f"in_{name}", v.shape, F32, kind="ExternalInput").ap() for name, v in arrays.items()}
    out = nc.dram_tensor("out", arrays["x"].shape, F32, kind="ExternalOutput").ap()
    hybrid_trunk(nc, args, out)
    r = run_bass_kernel_spmd(nc, [{f"in_{name}": v for name, v in arrays.items()}], core_ids=[0])
    return r.results[0]["out"]
```
